# Optimizing a Trainium2 kernel written in Bass

```python
import jax, jax.numpy as jnp
from jax import lax
import numpy as np

D_MODEL = 2048
BATCH = 1
SEQ = 256
DEPTH = 2

N_MIXERS = 2
GRID_W = 64
NORM_EPS = 1e-6

MLSTM_HEADS = 4
MLSTM_V_DIM = D_MODEL // MLSTM_HEADS
MLSTM_QK_DIM = MLSTM_V_DIM // 2
MLSTM_CHUNK = 128
MLSTM_F_BIAS_LO = 3.0
MLSTM_F_BIAS_HI = 6.0
MLSTM_IN = 2 * MLSTM_HEADS * MLSTM_QK_DIM + 2 * MLSTM_HEADS * MLSTM_V_DIM + 4 * MLSTM_HEADS

ATTN_HEAD_DIM = 128
ATTN_Q_HEADS = D_MODEL // ATTN_HEAD_DIM
ATTN_KV_HEADS = 4
ATTN_GROUPS = ATTN_Q_HEADS // ATTN_KV_HEADS
ATTN_Q_BLOCK = 128
ROPE_THETA = 10000.0
ATTN_IN = (ATTN_Q_HEADS + 2 * ATTN_KV_HEADS) * ATTN_HEAD_DIM

PEER_HEADS = 8
PEER_N_KEYS = 128
PEER_EXPERTS = PEER_N_KEYS ** 2
PEER_TOPK = 16
PEER_QUERY_DIM = 256
PEER_HALF = PEER_QUERY_DIM // 2
PEER_TOKEN_BLOCK = 128
PEER_V_SCALE = PEER_HEADS ** -0.5

kernel_name = "hybrid_mlstm_axialgqa_peer_encoder"

def rms_norm(x, g):
    xf = x.astype(jnp.float32)
    y = xf * lax.rsqrt(jnp.mean(xf * xf, axis=-1, keepdims=True) + NORM_EPS)
    return (y * g.astype(jnp.float32)).astype(x.dtype)

def mlstm_chunkwise(q, k, v, ig, fg):
    B, H, S, dk = q.shape
    dv = v.shape[-1]
    L = MLSTM_CHUNK
    nc = S // L

    def chunks(a):
        return jnp.moveaxis(a.reshape(B, H, nc, L, *a.shape[3:]), 2, 0)

    lower = jnp.tril(jnp.ones((L, L), dtype=bool))

    def step(carry, inp):
        C, n, m = carry
        q_, k_, v_, i_, f_ = inp
        b = jnp.cumsum(jax.nn.log_sigmoid(f_), axis=-1)
        log_d = jnp.where(lower, b[..., :, None] - b[..., None, :] + i_[..., None, :], -jnp.inf)
        m_inter = b + m[..., None]
        m_t = jnp.maximum(m_inter, jnp.max(log_d, axis=-1))
        dmat = jnp.exp(log_d - m_t[..., None])
        inter = jnp.exp(m_inter - m_t)
        s = jnp.einsum('bhtd,bhsd->bhts', q_, k_) * dmat
        num = jnp.einsum('bhts,bhsv->bhtv', s, v_) + inter[..., None] * jnp.einsum('bhvd,bhtd->bhtv', C, q_)
        den = jnp.sum(s, axis=-1) + inter * jnp.einsum('bhd,bhtd->bht', n, q_)
        h = num / jnp.maximum(jnp.abs(den), jnp.exp(-m_t))[..., None]
        b_last = b[..., -1]
        log_w = b_last[..., None] - b + i_
        m_new = jnp.maximum(b_last + m, jnp.max(log_w, axis=-1))
        w = jnp.exp(log_w - m_new[..., None])
        decay = jnp.exp(b_last + m - m_new)
        C = decay[..., None, None] * C + jnp.einsum('bhs,bhsv,bhsd->bhvd', w, v_, k_)
        n = decay[..., None] * n + jnp.einsum('bhs,bhsd->bhd', w, k_)
        return (C, n, m_new), h

    init = (jnp.zeros((B, H, dv, dk), jnp.float32),
            jnp.zeros((B, H, dk), jnp.float32),
            jnp.zeros((B, H), jnp.float32))
    _, h = lax.scan(step, init, (chunks(q), chunks(k), chunks(v), chunks(ig), chunks(fg)))
    return jnp.moveaxis(h, 0, 2).reshape(B, H, S, dv)

def mlstm_mixer(xn, w_in, gate_bias, head_norm, w_out):
    B, S, _ = xn.shape
    H = MLSTM_HEADS
    nqk = H * MLSTM_QK_DIM
    nv = H * MLSTM_V_DIM
    proj = xn @ w_in
    q, k, v, o, gates = jnp.split(proj, [nqk, 2 * nqk, 2 * nqk + nv, 2 * nqk + 2 * nv], axis=-1)

    def heads(a, d):
        return a.reshape(B, S, H, d).transpose(0, 2, 1, 3).astype(jnp.float32)

    q = heads(q, MLSTM_QK_DIM) * (MLSTM_QK_DIM ** -0.5)
    k = heads(k, MLSTM_QK_DIM)
    v = heads(v, MLSTM_V_DIM)
    g = (gates.reshape(B, S, 4, H).astype(jnp.float32) + gate_bias.astype(jnp.float32)).transpose(2, 0, 3, 1)
    h_fwd = mlstm_chunkwise(q, k, v, g[0], g[1])
    flip = lambda a: jnp.flip(a, axis=2)
    h_bwd = flip(mlstm_chunkwise(flip(q), flip(k), flip(v), flip(g[2]), flip(g[3])))
    h = h_fwd + h_bwd
    h = h * lax.rsqrt(jnp.mean(h * h, axis=-1, keepdims=True) + NORM_EPS) * head_norm.astype(jnp.float32)[None, :, None, :]
    h = h.transpose(0, 2, 1, 3).reshape(B, S, nv) * jax.nn.sigmoid(o.astype(jnp.float32))
    return h.astype(xn.dtype) @ w_out

def axial_rope(S):
    rows = S // GRID_W
    row = jnp.repeat(jnp.arange(rows, dtype=jnp.float32), GRID_W)
    col = jnp.tile(jnp.arange(GRID_W, dtype=jnp.float32), rows)
    n_freq = ATTN_HEAD_DIM // 4
    freqs = ROPE_THETA ** (-jnp.arange(n_freq, dtype=jnp.float32) / n_freq)
    ang = jnp.concatenate([row[:, None] * freqs, col[:, None] * freqs], axis=-1)
    return jnp.cos(ang), jnp.sin(ang)

def apply_rope(x, cos, sin):
    xp = x.reshape(*x.shape[:-1], -1, 2)
    x1, x2 = xp[..., 0], xp[..., 1]
    c = cos[None, :, None, :]
    s = sin[None, :, None, :]
    return jnp.stack([x1 * c - x2 * s, x1 * s + x2 * c], axis=-1).reshape(x.shape)

def attn_mixer(xn, w_in, q_norm, k_norm, w_out):
    B, S, _ = xn.shape
    nq = ATTN_Q_HEADS * ATTN_HEAD_DIM
    nkv = ATTN_KV_HEADS * ATTN_HEAD_DIM
    proj = xn @ w_in
    q, k, v = jnp.split(proj, [nq, nq + nkv], axis=-1)
    cos, sin = axial_rope(S)
    q = apply_rope(rms_norm(q.reshape(B, S, ATTN_Q_HEADS, ATTN_HEAD_DIM), q_norm).astype(jnp.float32), cos, sin)
    k = apply_rope(rms_norm(k.reshape(B, S, ATTN_KV_HEADS, ATTN_HEAD_DIM), k_norm).astype(jnp.float32), cos, sin)
    q = (q * (ATTN_HEAD_DIM ** -0.5)).astype(xn.dtype)
    k = k.astype(xn.dtype)
    v = v.reshape(B, S, ATTN_KV_HEADS, ATTN_HEAD_DIM)
    nb = S // ATTN_Q_BLOCK
    qb = jnp.moveaxis(q.reshape(B, nb, ATTN_Q_BLOCK, ATTN_KV_HEADS, ATTN_GROUPS, ATTN_HEAD_DIM), 1, 0)

    def block(q_blk):
        s = jnp.einsum('bqkgd,bskd->bkgqs', q_blk, k, preferred_element_type=jnp.float32)
        p = jax.nn.softmax(s, axis=-1).astype(v.dtype)
        return jnp.einsum('bkgqs,bskd->bqkgd', p, v)

    o = lax.map(block, qb)
    o = jnp.moveaxis(o, 0, 1).reshape(B, S, nq)
    return o @ w_out

def peer(xn, wq, k1, k2, u, v):
    B, S, D = xn.shape
    q = (xn @ wq).reshape(B, S, PEER_HEADS, 2, PEER_HALF)
    s1 = jnp.einsum('bshd,nd->bshn', q[..., 0, :], k1, preferred_element_type=jnp.float32)
    s2 = jnp.einsum('bshd,nd->bshn', q[..., 1, :], k2, preferred_element_type=jnp.float32)
    t1, i1 = lax.top_k(s1, PEER_TOPK)
    t2, i2 = lax.top_k(s2, PEER_TOPK)
    cand_s = (t1[..., :, None] + t2[..., None, :]).reshape(B, S, PEER_HEADS, PEER_TOPK * PEER_TOPK)
    cand_i = (i1[..., :, None] * PEER_N_KEYS + i2[..., None, :]).reshape(B, S, PEER_HEADS, PEER_TOPK * PEER_TOPK)
    top_s, pos = lax.top_k(cand_s, PEER_TOPK)
    idx = jnp.take_along_axis(cand_i, pos, axis=-1)
    gate = jax.nn.softmax(top_s, axis=-1)
    nblk = (B * S) // PEER_TOKEN_BLOCK
    E = PEER_HEADS * PEER_TOPK
    xb = xn.reshape(nblk, PEER_TOKEN_BLOCK, D)
    ib = idx.reshape(nblk, PEER_TOKEN_BLOCK, E)
    gb = gate.reshape(nblk, PEER_TOKEN_BLOCK, E)

    def block(args):
        x_blk, i_blk, g_blk = args
        act = jax.nn.gelu(jnp.einsum('td,ted->te', x_blk, u[i_blk], preferred_element_type=jnp.float32))
        return jnp.einsum('te,ted->td', (g_blk * act).astype(v.dtype), v[i_blk])

    return lax.map(block, (xb, ib, gb)).reshape(B, S, D)

def setup_inputs(seed: int = 0) -> dict:
    key = jax.random.key(seed)
    ks = jax.random.split(key, 17)
    n_a = (DEPTH + N_MIXERS - 1) // N_MIXERS
    n_b = DEPTH // N_MIXERS
    f32 = jnp.float32
    nrm = lambda k, shape, scale: jax.random.normal(k, shape, f32) * scale
    gain = lambda k, shape: 1.0 + 0.05 * jax.random.normal(k, shape, f32)
    nq = ATTN_Q_HEADS * ATTN_HEAD_DIM
    f_bias = jnp.linspace(MLSTM_F_BIAS_LO, MLSTM_F_BIAS_HI, MLSTM_HEADS, dtype=f32)
    base = jnp.array([0.0, 1.0, 0.0, 1.0], f32)[:, None] * f_bias[None, :]
    return {
        'x': nrm(ks[0], (BATCH, SEQ, D_MODEL), 1.0),
        'ln_mix': gain(ks[1], (DEPTH, D_MODEL)),
        'ln_ffn': gain(ks[2], (DEPTH, D_MODEL)),
        'mlstm_w_in': nrm(ks[3], (n_a, D_MODEL, MLSTM_IN), D_MODEL ** -0.5),
        'mlstm_gate_bias': base[None] + nrm(ks[4], (n_a, 4, MLSTM_HEADS), 0.1),
        'mlstm_head_norm': gain(ks[5], (n_a, MLSTM_HEADS, MLSTM_V_DIM)),
        'mlstm_w_out': nrm(ks[6], (n_a, MLSTM_HEADS * MLSTM_V_DIM, D_MODEL), (MLSTM_HEADS * MLSTM_V_DIM) ** -0.5),
        'attn_w_in': nrm(ks[7], (n_b, D_MODEL, ATTN_IN), D_MODEL ** -0.5),
        'attn_q_norm': gain(ks[8], (n_b, ATTN_HEAD_DIM)),
        'attn_k_norm': gain(ks[9], (n_b, ATTN_HEAD_DIM)),
        'attn_w_out': nrm(ks[10], (n_b, nq, D_MODEL), nq ** -0.5),
        'peer_wq': nrm(ks[11], (DEPTH, D_MODEL, PEER_HEADS * PEER_QUERY_DIM), D_MODEL ** -0.5),
        'peer_k1': nrm(ks[12], (DEPTH, PEER_N_KEYS, PEER_HALF), PEER_HALF ** -0.5),
        'peer_k2': nrm(ks[13], (DEPTH, PEER_N_KEYS, PEER_HALF), PEER_HALF ** -0.5),
        'peer_u': nrm(ks[14], (DEPTH, PEER_EXPERTS, D_MODEL), D_MODEL ** -0.5),
        'peer_v': nrm(ks[15], (DEPTH, PEER_EXPERTS, D_MODEL), PEER_V_SCALE),
    }

def reference(x, ln_mix, ln_ffn, mlstm_w_in, mlstm_gate_bias, mlstm_head_norm, mlstm_w_out,
              attn_w_in, attn_q_norm, attn_k_norm, attn_w_out,
              peer_wq, peer_k1, peer_k2, peer_u, peer_v):
    for layer in range(DEPTH):
        j = layer // N_MIXERS
        h = rms_norm(x, ln_mix[layer])
        if layer % N_MIXERS == 0:
            x = x + mlstm_mixer(h, mlstm_w_in[j], mlstm_gate_bias[j], mlstm_head_norm[j], mlstm_w_out[j])
        else:
            x = x + attn_mixer(h, attn_w_in[j], attn_q_norm[j], attn_k_norm[j], attn_w_out[j])
        h = rms_norm(x, ln_ffn[layer])
        x = x + peer(h, peer_wq[layer], peer_k1[layer], peer_k2[layer], peer_u[layer], peer_v[layer])
    return x


_drawn_inputs = setup_inputs


def setup_inputs(seed=0):
    import zlib

    import numpy as np

    out = dict(_drawn_inputs(seed))
    spreads = {}
    factors = {'attn_q_norm': 4.857, 'attn_k_norm': 4.643}
    for name, (base, spread) in spreads.items():
        noise = np.random.default_rng([zlib.crc32(name.encode()), seed]).standard_normal(out[name].shape)
        drawn = base * np.exp(spread * noise) if base else spread * noise
        out[name] = __import__('jax').numpy.asarray(drawn.astype(out[name].dtype))
    for name, factor in factors.items():
        out[name] = (out[name] * factor).astype(out[name].dtype)
    return out
```

```python
import concourse.bass as bass
from concourse import mybir
from contextlib import ExitStack
import numpy as np

F32 = mybir.dt.float32
U32 = mybir.dt.uint32
ALU = mybir.AluOpType
ACT = mybir.ActivationFunctionType
AX = mybir.AxisListType

P = 128
GRID_W = 64
EPS = 1e-6
ROPE_THETA = 10000.0
MASKED = -1e30
GELU_C = float(np.sqrt(2.0 / np.pi))
GELU_A = 0.044715

C_ID, C_IOTA, C_POW = 0, 128, 144
C_COS = C_POW + 8
C_SIN = C_COS + 256
C_KEPT = C_SIN + 128
M_TRI, M_ONES, M_MASK = 0, 256, 384
M_SEL = M_MASK + 4 * 256
M_ALL = M_SEL + 8 * 128
C_TRI, C_ONES, C_MASK, C_SEL = (C_KEPT + m for m in (M_TRI, M_ONES, M_MASK, M_SEL))
C_ALL = C_KEPT + M_ALL


def constants():
    c = np.zeros((P, C_ALL), np.float32)
    r = np.arange(P)
    c[:, C_ID:C_ID + P] = np.eye(P)
    c[:, C_TRI:C_TRI + P] = r[:, None] <= r[None, :]
    c[:, C_TRI + P:C_TRI + 2 * P] = r[:, None] >= r[None, :]
    c[:, C_ONES:C_ONES + P] = 1.0
    s = np.arange(2 * P)
    for d in range(2):
        for b in range(2):
            t = (b * P + r)[:, None]
            seen = (s[None, :] <= t) if d == 0 else (s[None, :] >= t)
            at = C_MASK + (2 * d + b) * 256
            c[:, at:at + 256] = np.where(seen, 0.0, MASKED)
    c[:, C_IOTA:C_IOTA + 16] = np.arange(16)
    n_freq = P // 4
    freqs = (np.float32(ROPE_THETA) ** (-np.arange(n_freq, dtype=np.float32) / np.float32(n_freq))).astype(np.float32)
    for b in range(2):
        t = b * P + r
        row, col = (t // GRID_W).astype(np.float32), (t % GRID_W).astype(np.float32)
        ang = np.concatenate([row[:, None] * freqs, col[:, None] * freqs], axis=-1).astype(np.float32)
        c[:, C_COS + b * P:C_COS + (b + 1) * P] = np.repeat(np.cos(ang), 2, axis=-1)
        c[:, C_SIN + b * 64:C_SIN + (b + 1) * 64] = np.sin(ang)
    for i in range(8):
        c[i, C_SEL + i * P:C_SEL + (i + 1) * P] = 1.0
    c[:, C_POW:C_POW + 8] = -0.5
    return c


class Steps:

    def __init__(self, eng, sem):
        self.eng, self.sem, self.n, self.loop = eng, sem, 0, 0

    def did(self, ins):
        self.n += 1
        ins.then_inc(self.sem, 1)
        return self.loop + self.n

    def need(self, count):
        self.eng.wait_ge(self.sem, count)


def trunk_kernel(nc, consts, x, ln_mix, ln_ffn, m_w_in, m_gate_bias, m_head_norm, m_w_out,
                 a_w_in, a_q_norm, a_k_norm, a_w_out, wq, k1T, k2T, u_tab, v_tab, out):
    D = x.shape[-1]
    KT = D // P
    NB = x.shape[1] // P
    T = NB * P
    M_HEADS, M_V = m_head_norm.shape[1:]
    M_QK = M_V // 2
    NQK, NV = M_HEADS * M_QK, M_HEADS * M_V
    DH = a_q_norm.shape[-1]
    A_HEADS = a_w_out.shape[1] // DH
    A_KV = (a_w_in.shape[2] // DH - A_HEADS) // 2
    HEADS = wq.shape[2] // (2 * P)
    TOPK = 16
    CH = 512
    QK = KT // 4
    SLOT = QK * CH
    NU, NVS = 4, 8
    UNITS = NB * HEADS
    assert SLOT == D and NB == 2 and T == 256 and M_V == CH and DH == P

    with ExitStack() as ctx:
        def sb(name, cols, dt=F32, rows=P):
            return ctx.enter_context(nc.sbuf_tensor(name, [rows, cols], dt))

        def sem(name):
            return ctx.enter_context(nc.semaphore(name))

        const = sb("const", C_KEPT)
        shared = sb("shared", 3072)
        x_sb = sb("x_sb", NB * D)
        actT_sb = sb("actT_sb", KT * T)
        ring_sb = sb("ring_sb", (NU + NVS) * SLOT)
        arena = sb("arena", 3 * NB * D)
        gain = sb("gain", D)
        w_gate = sb("w_gate", KT * 16)
        bias = sb("bias", 16)
        small = sb("small", 40)
        keysT = sb("keysT", 2 * P)
        qkgain = sb("qkgain", 2 * P)

        ident = const[:, C_ID:C_ID + P]
        tri = [shared[:, M_TRI + d * P:M_TRI + (d + 1) * P] for d in range(2)]
        ones = shared[:, M_ONES:M_ONES + P]
        iota = const[:, C_IOTA:C_IOTA + 16]
        xb = [x_sb[:, b * D:(b + 1) * D] for b in range(NB)]
        actT = actT_sb[:, :].rearrange("p (k t) -> p k t", t=T)
        ring = [ring_sb[:, s * SLOT:(s + 1) * SLOT] for s in range(NU + NVS)]
        xn = [arena[:, b * D:(b + 1) * D] for b in range(NB)]
        ssq, ms, rstd = small[:, 0:2], small[:, 8:10], small[:, 16:18]

        EXPERTS = u_tab.shape[1]
        u_rows, v_rows = (t.rearrange("l e d -> (l e) d") for t in (u_tab, v_tab))

        banks = [ctx.enter_context(nc.psum_tensor(f"bank{i}", [P, CH], F32)) for i in range(8)]
        acc, trb, mis = banks[0:4], banks[4:6], banks[6:8]

        consts_in, x_in, gain_in = sem("consts_in"), sem("x_in"), sem("gain_in")
        keys_in, wg_in, qkg_in = sem("keys_in"), sem("wg_in"), sem("qkg_in")
        dve_done, act_done = sem("dve_done"), sem("act_done")
        ssq_ready, ms_ready, rstd_ready, xn_ready = sem("ssq_ready"), sem("ms_ready"), sem("rstd_ready"), sem("xn_ready")
        tr_full = [sem("tr_full_act"), sem("tr_full_dve")]
        tr_out = [sem("tr_out_act"), sem("tr_out_dve")]
        w_landed = [sem(f"w_landed{s}") for s in range(8)]
        w_used = sem("w_used")
        acc_out = sem("acc_out")
        gates_full, exp_in, exp_out, ls_ready, cum_full = (sem(n) for n in ("gates_full", "exp_in", "exp_out", "ls_ready", "cum_full"))
        a_ready, bc_full, bc_used = sem("a_ready"), sem("bc_full"), sem("bc_used")
        negm_ready, en_ready, decay_ready = sem("negm_ready"), sem("en_ready"), sem("decay_ready")
        s_full, s_used, p_ready = sem("s_full"), sem("s_used"), sem("p_ready")
        h_full, h_out, msh_ready, rh_ready, h_ready = (sem(n) for n in ("h_full", "h_out", "msh_ready", "rh_ready", "h_ready"))
        sq_ready, msq_ready, rq_ready, qk_ready = (sem(n) for n in ("sq_ready", "msq_ready", "rq_ready", "qk_ready"))
        as_full, amax_ready, ap_ready, an_ready, o_full, o_out = (sem(n) for n in ("as_full", "amax_ready", "ap_ready", "an_ready", "o_full", "o_out"))
        wq_landed = [sem("wq_landed0"), sem("wq_landed1")]
        rq_full, rq_out, rt_full, rt_out, sc_full, sc_out = (sem(n) for n in ("rq_full", "rq_out", "rt_full", "rt_out", "sc_full", "sc_out"))
        top_ready, gexp_ready, idx_ready, idx_taken = (sem(n) for n in ("top_ready", "gexp_ready", "idx_ready", "idx_taken"))
        u_landed = [sem(f"u_landed{s}") for s in range(NU)]
        v_landed = [sem(f"v_landed{s}") for s in range(NVS)]
        u_used = sem("u_used")
        v_used = sem("v_used")
        tanh_in, tanh_out, w_ready, diag_ready = sem("tanh_in"), sem("tanh_out"), sem("w_ready"), sem("diag_ready")
        x_out, stored = sem("x_out"), sem("stored")

        mproj = arena[:, :].rearrange("p (b n) -> p b n", b=NB)
        m_v = mproj[:, :, 2 * NQK:2 * NQK + NV]
        m_o = mproj[:, :, 2 * NQK + NV:2 * NQK + 2 * NV]
        m_h = mproj[:, :, 0:NV]
        m_qkT = ring_sb[:, 8 * SLOT:10 * SLOT].rearrange("p (k t) -> p k t", t=T)
        m_D = ring_sb[:, 10 * SLOT:12 * SLOT].rearrange("p (u t) -> p u t", t=T)
        m_PT = actT_sb[:, 0:M_HEADS * 2 * T].rearrange("p (h s t) -> p h s t", h=M_HEADS, s=NB)
        g_sb, gf, ge, gd, gr, gz, gz2, gp = (sb(f"gate{i}", 32) for i in range(8))
        gls, ga, gB = sb("gls", 16), sb("ga", 16), sb("gB", 16)
        aT = sb("aT", T, rows=8)
        m_M, m_negM, m_nm, m_en, m_den, m_dn, m_rr = (sb(f"m_stat{i}", 16) for i in range(7))
        h_ssq, h_ms, h_r = sb("h_ssq", 8), sb("h_ms", 8), sb("h_r", 8)
        h_junk = actT_sb[:, 2048:2048 + CH]

        aproj = arena[:, 0:NB * 3072].rearrange("p (b n) -> p b n", b=NB)
        a_sq = arena[:, 6144:7168]
        a_y = arena[:, 7168:8192].rearrange("p (b h d) -> p b h d", b=NB, d=DH)
        a_t1 = arena[:, 8192:9216].rearrange("p (b h d) -> p b h d", b=NB, d=DH)
        a_t2 = arena[:, 9216:10240].rearrange("p (b h d) -> p b h d", b=NB, d=DH)
        a_kT = ring[8][:, 0:A_KV * T].rearrange("p (k t) -> p k t", t=T)
        a_P = [ring[9][:, i * 512:(i + 1) * 512].rearrange("p (b s) -> p b s", b=NB) for i in range(2)]
        a_PT = [ring[10][:, i * 512:(i + 1) * 512].rearrange("p (s t) -> p s t", s=NB) for i in range(2)]
        a_mx, a_nmx, a_sum, a_rs = (sb(f"a_stat{i}", 4) for i in range(4))
        q_ssq, q_ms, q_r = sb("q_ssq", 8), sb("q_ms", 8), sb("q_r", 8)

        scores = arena[:, 2 * D:4 * D]
        scores_bh = scores.rearrange("p (b r) -> p b r", b=NB)
        wq_slot = [arena[:, (4 + i) * D:(5 + i) * D].rearrange("p (k n) -> p k n", n=2 * P) for i in range(2)]
        taken = [0]

        def tile(cols, dt=F32):
            taken[0] += cols
            assert taken[0] <= 3072
            t = shared[:, taken[0] - cols:taken[0]]
            return t.bitcast(dt) if dt is not F32 else t

        q_nat, q_T, onehot = tile(2 * 2 * P), tile(2 * 2 * P), tile(512)
        scur, srep, cand, crep = tile(2 * P), tile(2 * P), tile(256), tile(256)
        t_val, t_idx, t_idf = tile(32), tile(32, U32), tile(32)
        c_top, c_pos, c_ab, sel_if = tile(16), tile(16, U32), tile(32, U32), tile(32)
        negmax, g_exp, g_sum, g_rec, gate_next, gate_cur = tile(1), tile(16), tile(1), tile(1), tile(16), tile(16)
        idx_next = sb("idx_next", 16, U32)
        idx_cur = [sb("idx_cur0", 16, U32), sb("idx_cur1", 16, U32)]
        dots, e_x2, e_t, e_in, e_th, e_p, e_w = (tile(16) for i in range(7))
        diag = [sb(f"diag{i}", P) for i in range(4)]
        u_slot, v_slot = ring[0:NU], ring[NU:NU + NVS]

        GR = {}
        n_groups = 0
        for name, n in (("n0", 8), ("qk", 8), ("a", 1), ("pt", M_HEADS), ("h", 8), ("n1", 8), ("n2", 8),
                        ("akT", 2), ("aqT", 8), ("apt", A_HEADS), ("n3", 8)):
            GR[name] = n_groups
            n_groups += n

        def group_filled(pe, g):
            return tr_full[g % 2]

        def wait_bank(pe, g):
            if g >= 2:
                pe.wait_ge(tr_out[g % 2], g // 2)

        def wait_groups(eng, first, n):
            for par in range(2):
                last = max((g for g in range(first, first + n) if g % 2 == par), default=None)
                if last is not None:
                    eng.wait_ge(tr_out[par], last // 2 + 1)

        def copy_group(eng, copy, g, dst, cols=512, rows=P):
            eng.wait_ge(tr_full[g % 2], g // 2 + 1)
            src = trb[g % 2][0:rows, 0:cols]
            if len(dst.shape) == 3:
                src = src.rearrange("p (k t) -> p k t", t=dst.shape[2])
            copy(dst, src).then_inc(tr_out[g % 2], 1)

        def norm_dst(g):
            b, q = g // 4, g % 4
            return actT[:, 4 * q:4 * q + 4, b * P:(b + 1) * P]

        def qkT_dst(g):
            return m_qkT[:, 2 * g:2 * g + 2, :]

        W_CH = {"m_in": (0, 12), "m_out": (12, 4), "a_in": (16, 6), "a_out": (22, 4)}
        M_CHUNKS = 16
        ALL_CHUNKS = 26

        waits_passed = {"pool": sem("pool_waits_passed"), "dve": sem("dve_waits_passed")}

        def settle(eng):
            eng.sem_inc(waits_passed["pool" if eng is pool_engine[0] else "dve"], 1)

        pool_engine = [None]
        block = ctx.enter_context(nc.Block())

        @block.sync
        def _(sp):
            sp.dma_start(const[:, :], consts[:, 0:C_KEPT]).then_inc(consts_in, 16)
            sp.dma_start(shared[:, 0:M_ALL], consts[:, C_KEPT:C_ALL]).then_inc(wg_in, 16)
            for b in range(NB):
                sp.dma_start(xb[b], x[0, b * P:(b + 1) * P, :]).then_inc(x_in, 16)
            sp.dma_start(w_gate[:, :].rearrange("p (k n) -> p k n", n=16),
                         m_w_in[0, :, 2 * NQK + 2 * NV:].rearrange("(k p) n -> p k n", p=P)).then_inc(wg_in, 16)
            sp.dma_start(bias[:, :], m_gate_bias[0].rearrange("t h -> (t h)").partition_broadcast(P)).then_inc(wg_in, 16)

            def load_chunks(w, first, n):
                with sp.Fori(0, n // 2) as pair:
                    for par in range(2):
                        for j in range(4):
                            c4 = pair * 8 + (4 * (first + par) + j + 1)
                            sp.wait_ge(w_used, c4)
                            src = w[j * CH:(j + 1) * CH, bass.ds(pair * (2 * CH) + par * CH, CH)]
                            sp.dma_start(ring[4 * par + j].rearrange("p (k n) -> p k n", n=CH),
                                         src.rearrange("(k p) n -> p k n", p=P)).then_inc(w_landed[4 * par + j], 16)

            def load_queries(l):
                keys = [k1T, k2T]
                for i in range(2):
                    if l:
                        sp.wait_ge(sc_out, HEADS)
                    sp.dma_start(keysT[:, i * P:(i + 1) * P], keys[i][l]).then_inc(keys_in, 16)
                half = D // 2

                def load(h):
                    for i in range(2):
                        sp.dma_start(wq_slot[i], wq[l, i * half:(i + 1) * half, bass.ds(h * (2 * P), 2 * P)]
                                     .rearrange("(k p) n -> p k n", p=P)).then_inc(wq_landed[i], 16)
                load(0)
                with sp.Fori(1, HEADS) as h:
                    sp.wait_ge(rq_full, h + l * HEADS)
                    load(h)

            load_chunks(m_w_in[0], *W_CH["m_in"])
            load_chunks(m_w_out[0], *W_CH["m_out"])
            sp.wait_ge(h_ready, 8)
            load_queries(0)
            sp.wait_ge(u_used, NU + UNITS * TOPK)
            sp.wait_ge(v_used, NVS + UNITS * TOPK)
            for i, g in enumerate((a_q_norm, a_k_norm)):
                sp.dma_start(qkgain[:, i * P:(i + 1) * P], g[0].partition_broadcast(P)).then_inc(qkg_in, 16)
            load_chunks(a_w_in[0], *W_CH["a_in"])
            load_chunks(a_w_out[0], *W_CH["a_out"])
            sp.wait_ge(o_full, A_HEADS)
            load_queries(1)
            for b in range(NB):
                sp.wait_ge(x_out, 4 * (NB + b + 1))
                sp.dma_start(out[0, b * P:(b + 1) * P, :], xb[b]).then_inc(stored, 16)
            sp.wait_ge(stored, 16 * NB)

        @block.gpsimd
        def _(pool):
            pool_engine[0] = pool
            pool.wait_ge(consts_in, 16)
            minus_half = const[:, C_POW:C_POW + 8]

            def rsqrt_of(out_, in_, n):
                return nc.gpsimd.tensor_tensor(out_, in_, minus_half[:, 0:n], ALU.pow)

            def norm(s):
                pool.wait_ge(ms_ready, s + 1)
                rsqrt_of(rstd, ms, 2).then_inc(rstd_ready, 1)

            def gathers(l):
                pool.wait_ge(w_used, 8 + 4 * (M_CHUNKS if l == 0 else ALL_CHUNKS))
                if l:
                    pool.wait_ge(acc_out, 4 + 2 * ALL_CHUNKS)
                with pool.Fori(0, UNITS // 2) as pair:
                    for par in range(2):
                        gu = pair * 2 + (l * UNITS + par)
                        pool.wait_ge(idx_ready, gu + 1)
                        settle(pool)
                        nc.gpsimd.tensor_copy(idx_cur[par][:, :], idx_next[:, :]).then_inc(idx_taken, 1)
                        pool.wait_ge(idx_taken, gu + 1)
                        for k in range(TOPK):
                            pool.wait_ge(u_used, gu * TOPK + (k + 1))
                            settle(pool)
                            nc.gpsimd.indirect_dma_start(
                                out=u_slot[k % NU], out_offset=None, in_=u_rows,
                                in_offset=bass.IndirectOffsetOnAxis(ap=idx_cur[par][:, k:k + 1], axis=0),
                            ).then_inc(u_landed[k % NU], 16)
                            pool.wait_ge(v_used, gu * TOPK + (k + 1))
                            settle(pool)
                            nc.gpsimd.indirect_dma_start(
                                out=v_slot[k % NVS], out_offset=None, in_=v_rows,
                                in_offset=bass.IndirectOffsetOnAxis(ap=idx_cur[par][:, k:k + 1], axis=0),
                            ).then_inc(v_landed[k % NVS], 16)

            norm(0)
            pool.wait_ge(msh_ready, 1)
            rsqrt_of(h_r[:, :], h_ms[:, :], 8).then_inc(rh_ready, 1)
            norm(1)
            gathers(0)
            norm(2)
            for c in range(5):
                pool.wait_ge(msq_ready, c + 1)
                rsqrt_of(q_r[:, :], q_ms[:, :], 8).then_inc(rq_ready, 1)
            norm(3)
            gathers(1)

        @block.scalar
        def _(act):
            st = Steps(act, act_done)
            copy = nc.scalar.copy
            act.sem_inc(acc_out, 4)
            gains = [ln_mix[0], m_head_norm[0].rearrange("h v -> (h v)"), ln_ffn[0], ln_mix[1], ln_ffn[1]]

            def load_gain(i):
                act.dma_start(gain[:, :], gains[i].partition_broadcast(P)).then_inc(gain_in, 16)

            def norm(s, name):
                for b in range(NB):
                    if s == 0:
                        act.wait_ge(x_in, 16 * NB)
                    elif s % 2 == 1:
                        act.wait_ge(acc_out, 4 + 2 * (M_CHUNKS if s == 1 else ALL_CHUNKS))
                    else:
                        act.wait_ge(x_out, 4 * NB * (s // 2))
                    nc.scalar.activation(actT_sb[:, b * D:(b + 1) * D], xb[b], ACT.Square,
                                         accum_out=ssq[:, b:b + 1]).then_inc(ssq_ready, 1)
                for g in range(GR[name], GR[name] + 8):
                    if g % 2 == 0:
                        copy_group(act, copy, g, norm_dst(g - GR[name]))

            def project(dst, first, pair0, pair1, func=ACT.Copy):
                with act.Fori(pair0, pair1) as pair:
                    for par in range(2):
                        act.wait_ge(w_used, pair * 8 + (8 + 4 * (first + par) + 4))
                        for b in range(NB):
                            nc.scalar.activation(dst[:, b, bass.ds(pair * (2 * CH) + par * CH, CH)],
                                                 acc[2 * par + b][:, :], func).then_inc(acc_out, 1)

            load_gain(0)
            norm(0, "n0")
            act.wait_ge(xn_ready, 2)
            load_gain(1)
            act.wait_ge(exp_in, 1)
            nc.scalar.activation(ge[:, 0:16], gf[:, 0:16], ACT.Exp, scale=-1.0).then_inc(exp_out, 1)
            project(mproj, 0, 0, 2)
            for g in range(8):
                if (GR["qk"] + g) % 2 == 0:
                    copy_group(act, copy, GR["qk"] + g, qkT_dst(g))
            project(mproj, 0, 2, 3)
            copy_group(act, copy, GR["a"], aT[:, :], cols=T, rows=8)
            project(mproj, 0, 3, 4)
            act.wait_ge(negm_ready, 1)
            nc.scalar.activation(m_en[:, :], m_nm[:, :], ACT.Exp).then_inc(en_ready, 1)
            for i in range(16):
                nc.scalar.activation(m_D[:, i, :], m_D[:, i, :], ACT.Exp,
                                     bias=m_negM[:, i:i + 1]).then_inc(decay_ready, 1)
            project(mproj, 0, 4, 6, ACT.Sigmoid)
            for h in range(M_HEADS):
                if (GR["pt"] + h) % 2 == 0:
                    copy_group(act, copy, GR["pt"] + h, m_PT[:, h, :, :])
            for i in range(8):
                act.wait_ge(h_full, i + 1)
                head, b = i // 2, i % 2
                nc.scalar.copy(m_h[:, b, head * M_V:(head + 1) * M_V], acc[i % 4][:, :]).then_inc(h_out, 1)
                if i:
                    st.need(st.n)
                st.did(nc.scalar.activation(h_junk, acc[i % 4][:, :], ACT.Square, accum_out=h_ssq[:, i:i + 1]))
            for g in range(8):
                if (GR["h"] + g) % 2 == 0:
                    copy_group(act, copy, GR["h"] + g, norm_dst(g))

            def peer(l):
                def router(h):
                    n = h + l * HEADS
                    act.wait_ge(rq_full, n + 1)
                    nc.scalar.copy(q_nat[:, :], mis[0][:, :]).then_inc(rq_out, 1)
                    act.wait_ge(rt_full, n + 1)
                    nc.scalar.copy(q_T[:, :], trb[0][:, :]).then_inc(rt_out, 1)
                    act.wait_ge(sc_full, n + 1)
                    nc.scalar.copy(scores_bh[:, :, bass.ds(h * (2 * P), 2 * P)],
                                   mis[1][:, :].rearrange("p (b n) -> p b n", b=NB)).then_inc(sc_out, 1)

                def gate_exp(gu):
                    act.wait_ge(top_ready, gu + 1)
                    nc.scalar.activation(g_exp[:, :], c_top[:, :], ACT.Exp, bias=negmax[:, :],
                                         accum_out=g_sum[:, :]).then_inc(gexp_ready, 1)

                def unit(gu, more):
                    for j in range(4):
                        act.wait_ge(tanh_in, gu * 4 + (j + 1))
                        nc.scalar.activation(e_th[:, 4 * j:4 * j + 4], e_in[:, 4 * j:4 * j + 4], ACT.Tanh,
                                             scale=GELU_C).then_inc(tanh_out, 1)
                        act.wait_ge(w_ready, gu * 4 + (j + 5))
                        for k in range(4 * j, 4 * j + 4):
                            act.wait_ge(v_used, gu * TOPK + (k - 4 + NVS + 1))
                            nc.scalar.activation(diag[k % 4][:, :], ident, ACT.Copy,
                                                 scale=e_w[:, k:k + 1]).then_inc(diag_ready, 1)
                        if j == 1 and more:
                            gate_exp(gu + 1)

                def results(b):
                    act.wait_ge(v_used, NVS + (l * UNITS + (b + 1) * HEADS) * TOPK)
                    for n in range(4):
                        nc.scalar.copy(xb[b][:, n * CH:(n + 1) * CH], acc[n][:, :]).then_inc(x_out, 1)

                base = l * UNITS
                router(0)
                gate_exp(base)
                with act.Fori(0, HEADS - 1) as h:
                    router(h + 1)
                    unit(h + base, True)
                unit(base + HEADS - 1, True)
                results(0)
                with act.Fori(0, HEADS - 1) as h:
                    unit(h + (base + HEADS), True)
                unit(base + UNITS - 1, False)
                results(1)

            act.wait_ge(h_ready, 8)
            load_gain(2)
            norm(1, "n1")
            act.wait_ge(xn_ready, 4)
            load_gain(3)
            peer(0)

            norm(2, "n2")
            act.wait_ge(xn_ready, 6)
            load_gain(4)
            for c in range(5):
                par = c % 2
                act.wait_ge(w_used, 8 + 4 * (W_CH["a_in"][0] + c) + 4)
                if c:
                    act.wait_ge(msq_ready, c)
                for b in range(NB):
                    nc.scalar.activation(a_sq[:, b * CH:(b + 1) * CH], acc[2 * par + b][:, :],
                                         ACT.Square).then_inc(sq_ready, 1)
            act.wait_ge(w_used, 8 + 4 * (W_CH["a_in"][0] + 5) + 4)
            act.wait_ge(acc_out, 4 + 2 * (M_CHUNKS + 5))
            for b in range(NB):
                nc.scalar.copy(aproj[:, b, 5 * CH:6 * CH], acc[2 + b][:, :]).then_inc(acc_out, 1)
            for g in range(2):
                if (GR["akT"] + g) % 2 == 0:
                    copy_group(act, copy, GR["akT"] + g, a_kT[:, 2 * g:2 * g + 2, :])
            for g in range(8):
                if (GR["aqT"] + g) % 2 == 0:
                    copy_group(act, copy, GR["aqT"] + g, actT[:, 2 * g:2 * g + 2, :])
            for h in range(A_HEADS + 2):
                if h < A_HEADS:
                    act.wait_ge(amax_ready, h + 1)
                    if h >= 2:
                        act.wait_ge(tr_full[(GR["apt"] + h - 2) % 2], (GR["apt"] + h - 2) // 2 + 1)
                    for b in range(NB):
                        nc.scalar.activation(a_P[h % 2][:, b, :], mis[h % 2][:, b * T:(b + 1) * T], ACT.Exp,
                                             bias=a_nmx[:, 2 * (h % 2) + b:2 * (h % 2) + b + 1],
                                             accum_out=a_sum[:, 2 * (h % 2) + b:2 * (h % 2) + b + 1]).then_inc(ap_ready, 1)
                if 1 <= h <= A_HEADS and (GR["apt"] + h - 1) % 2 == 0:
                    if h >= 3:
                        act.wait_ge(o_full, h - 2)
                    copy_group(act, copy, GR["apt"] + h - 1, a_PT[(h - 1) % 2])
                if h >= 2:
                    act.wait_ge(o_full, h - 1)
                    nc.scalar.copy(actT[:, h - 2, :], acc[(h - 2) % 4][:, 0:T]).then_inc(o_out, 1)
            norm(3, "n3")
            peer(1)

        @block.tensor
        def _(pe):
            mm, tp = nc.tensor.matmul, nc.tensor.transpose
            pe.sem_inc(w_used, 8)
            pe.sem_inc(v_used, NVS)
            pe.wait_ge(consts_in, 16)

            def norm(s, name):
                for g in range(8):
                    b, q = g // 4, g % 4
                    pe.wait_ge(xn_ready, 2 * s + b + 1)
                    wait_bank(pe, GR[name] + g)
                    for i in range(4):
                        f = 4 * q + i
                        last = tp(trb[(GR[name] + g) % 2][:, i * P:(i + 1) * P], xn[b][:, f * P:(f + 1) * P], ident)
                    last.then_inc(tr_full[(GR[name] + g) % 2], 1)
                wait_groups(pe, GR[name], 8)

            def project(first, pair0, pair1):
                with pe.Fori(pair0, pair1) as pair:
                    for par in range(2):
                        for j in range(4):
                            pe.wait_ge(w_landed[4 * par + j], pair * 16 + (16 * (first // 2) + 16))
                            if j == 0:
                                pe.wait_ge(acc_out, pair * 4 + (2 * (first + par) + 2))
                            for b in range(NB):
                                for k in range(QK):
                                    last = mm(acc[2 * par + b][:, :], actT[:, QK * j + k, b * P:(b + 1) * P],
                                              ring[4 * par + j][:, k * CH:(k + 1) * CH],
                                              start=(j == 0 and k == 0), stop=(j == 3 and k == QK - 1),
                                              skip_group_check=True)
                            last.then_inc(w_used, 1)

            norm(0, "n0")
            pe.wait_ge(wg_in, 48)
            for b in range(NB):
                for k in range(KT):
                    last = mm(mis[0][:, b * 16:(b + 1) * 16], actT[:, k, b * P:(b + 1) * P],
                              w_gate[:, k * 16:(k + 1) * 16], start=(k == 0), stop=(k == KT - 1))
            last.then_inc(gates_full, 1)
            project(0, 0, 2)
            pe.wait_ge(ls_ready, 1)
            for b in range(NB):
                for d in range(2):
                    o = mis[1][:, b * 8 + d * 4:b * 8 + d * 4 + 4]
                    both = b == (1 if d == 0 else 0)
                    last = mm(o, tri[d], gls[:, b * 8 + d * 4:b * 8 + d * 4 + 4], start=True, stop=not both)
                    if both:
                        last = mm(o, ones, gls[:, (1 - b) * 8 + d * 4:(1 - b) * 8 + d * 4 + 4], start=False, stop=True)
            last.then_inc(cum_full, 1)
            pe.wait_ge(acc_out, 4 + 8)
            for g in range(8):
                wait_bank(pe, GR["qk"] + g)
                for i in range(4):
                    tile, b = 2 * g + i // 2, i % 2
                    last = tp(trb[(GR["qk"] + g) % 2][:, i * P:(i + 1) * P], mproj[:, b, tile * P:(tile + 1) * P], ident)
                last.then_inc(tr_full[(GR["qk"] + g) % 2], 1)
            project(0, 2, 3)
            pe.wait_ge(a_ready, 1)
            wait_bank(pe, GR["a"])
            for b in range(NB):
                last = tp(trb[GR["a"] % 2][0:8, b * P:(b + 1) * P], ga[:, b * 8:(b + 1) * 8], ident)
            last.then_inc(tr_full[GR["a"] % 2], 1)
            wait_groups(pe, GR["a"], 1)
            for i in range(8):
                if i >= 2:
                    pe.wait_ge(bc_used, 2 * (i - 1))
                mm(mis[i % 2][:, 0:T], shared[0:8, M_SEL + i * P:M_SEL + (i + 1) * P], aT[:, :],
                   start=True, stop=True).then_inc(bc_full, 1)
            project(0, 3, 4)
            wait_groups(pe, GR["qk"], 8)
            for i in range(8):
                head, b = i // 2, i % 2
                if i >= 2:
                    pe.wait_ge(s_used, 2 * (i - 1))
                elif i == 0:
                    pe.wait_ge(bc_used, 16)
                for d in range(M_QK // P):
                    last = mm(mis[i % 2][:, 0:T], m_qkT[:, 2 * head + d, b * P:(b + 1) * P],
                              m_qkT[:, NQK // P + 2 * head + d, :], start=(d == 0), stop=(d == M_QK // P - 1))
                last.then_inc(s_full, 1)
            project(0, 4, 6)
            for h in range(M_HEADS):
                wait_bank(pe, GR["pt"] + h)
                pe.wait_ge(p_ready, 2 * h + 2)
                for i in range(4):
                    s, b = i // 2, i % 2
                    last = tp(trb[(GR["pt"] + h) % 2][:, i * P:(i + 1) * P], m_D[:, 2 * h + b, s * P:(s + 1) * P], ident)
                last.then_inc(tr_full[(GR["pt"] + h) % 2], 1)
            pe.wait_ge(acc_out, 4 + 24)
            for i in range(8):
                head, b = i // 2, i % 2
                wait_groups(pe, GR["pt"] + head, 1)
                if i >= 4:
                    pe.wait_ge(h_out, i - 3)
                    pe.wait_ge(act_done, i - 3)
                for s in range(NB):
                    last = mm(acc[i % 4][:, :], m_PT[:, head, s, b * P:(b + 1) * P],
                              m_v[:, s, head * M_V:(head + 1) * M_V], start=(s == 0), stop=(s == NB - 1))
                last.then_inc(h_full, 1)
            for g in range(8):
                b, q = g // 4, g % 4
                pe.wait_ge(h_ready, 4 * b + q + 1)
                wait_bank(pe, GR["h"] + g)
                for i in range(4):
                    f = 4 * q + i
                    last = tp(trb[(GR["h"] + g) % 2][:, i * P:(i + 1) * P], m_h[:, b, f * P:(f + 1) * P], ident)
                last.then_inc(tr_full[(GR["h"] + g) % 2], 1)
            wait_groups(pe, GR["h"], 8)
            project(12, 0, 2)

            def peer(l):
                def router(h):
                    n = h + l * HEADS
                    for i in range(2):
                        pe.wait_ge(wq_landed[i], n * 16 + 16)
                    for b in range(NB):
                        for k in range(KT):
                            last = mm(mis[0][:, b * 2 * P:(b + 1) * 2 * P], actT[:, k, b * P:(b + 1) * P],
                                      wq_slot[k // 8][:, k % 8, :], start=(k == 0), stop=(k == KT - 1),
                                      skip_group_check=True)
                    last.then_inc(rq_full, 1)
                    pe.wait_ge(rq_out, n + 1)
                    for i in range(4):
                        side, b = i // 2, i % 2
                        last = tp(trb[0][:, i * P:(i + 1) * P],
                                  q_nat[:, (2 * b + side) * P:(2 * b + side + 1) * P], ident)
                    last.then_inc(rt_full, 1)
                    pe.wait_ge(rt_out, n + 1)
                    for i in range(4):
                        b, side = i // 2, i % 2
                        last = mm(mis[1][:, i * P:(i + 1) * P], q_T[:, (2 * side + b) * P:(2 * side + b + 1) * P],
                                  keysT[:, side * P:(side + 1) * P], start=True, stop=True, skip_group_check=True)
                    last.then_inc(sc_full, 1)

                def seed(b):
                    for n in range(4):
                        mm(acc[n][:, :], ident, xb[b][:, n * CH:(n + 1) * CH], start=True, stop=False,
                           skip_group_check=True)

                def unit(gu, end):
                    for k in range(TOPK):
                        pe.wait_ge(diag_ready, gu * TOPK + (k + 1))
                        pe.wait_ge(v_landed[k % NVS], gu * 32 + (16 * (k // NVS) + 16))
                        for n in range(4):
                            last = mm(acc[n][:, :], diag[k % 4][:, :], v_slot[k % NVS][:, n * CH:(n + 1) * CH],
                                      start=False, stop=end and k == TOPK - 1, skip_group_check=True)
                        last.then_inc(v_used, 1)

                base = l * UNITS
                pe.wait_ge(keys_in, 32 * (l + 1))
                router(0)
                seed(0)
                with pe.Fori(0, HEADS - 1) as h:
                    router(h + 1)
                    unit(h + base, False)
                unit(base + HEADS - 1, True)
                pe.wait_ge(x_out, 4 * (NB * l + 1))
                seed(1)
                with pe.Fori(0, HEADS - 1) as h:
                    unit(h + (base + HEADS), False)
                unit(base + UNITS - 1, True)

            norm(1, "n1")
            peer(0)

            norm(2, "n2")
            project(16, 0, 3)
            pe.wait_ge(qk_ready, 10)
            for g in range(2):
                wait_bank(pe, GR["akT"] + g)
                for i in range(4):
                    kv, b = 2 * g + i // 2, i % 2
                    last = tp(trb[(GR["akT"] + g) % 2][:, i * P:(i + 1) * P],
                              aproj[:, b, (A_HEADS + kv) * P:(A_HEADS + kv + 1) * P], ident)
                last.then_inc(tr_full[(GR["akT"] + g) % 2], 1)
            for g in range(8):
                wait_bank(pe, GR["aqT"] + g)
                for i in range(4):
                    h, b = 2 * g + i // 2, i % 2
                    last = tp(trb[(GR["aqT"] + g) % 2][:, i * P:(i + 1) * P], aproj[:, b, h * P:(h + 1) * P], ident)
                last.then_inc(tr_full[(GR["aqT"] + g) % 2], 1)
            wait_groups(pe, GR["akT"], 10)
            pe.wait_ge(acc_out, 4 + 2 * 22)

            def a_scores(h):
                if h >= 2:
                    pe.wait_ge(ap_ready, 2 * (h - 1))
                for b in range(NB):
                    last = mm(mis[h % 2][:, b * T:(b + 1) * T], actT[:, h, b * P:(b + 1) * P],
                              a_kT[:, h // (A_HEADS // A_KV), :], start=True, stop=True, skip_group_check=True)
                last.then_inc(as_full, 1)

            a_scores(0)
            a_scores(1)
            for h in range(A_HEADS):
                g = GR["apt"] + h
                pe.wait_ge(an_ready, 2 * h + 2)
                wait_bank(pe, g)
                for i in range(4):
                    s, b = i // 2, i % 2
                    last = tp(trb[g % 2][:, i * P:(i + 1) * P], a_P[h % 2][:, b, s * P:(s + 1) * P], ident)
                last.then_inc(tr_full[g % 2], 1)
                if h + 2 < A_HEADS:
                    a_scores(h + 2)
                wait_groups(pe, g, 1)
                if h >= 4:
                    pe.wait_ge(o_out, h - 3)
                kv = h // (A_HEADS // A_KV)
                for s in range(NB):
                    last = mm(acc[h % 4][:, 0:T], aproj[:, s, (A_HEADS + A_KV + kv) * P:(A_HEADS + A_KV + kv + 1) * P],
                              a_PT[h % 2][:, s, :], start=(s == 0), stop=(s == NB - 1))
                last.then_inc(o_full, 1)
            pe.wait_ge(o_out, A_HEADS)
            project(22, 0, 2)
            norm(3, "n3")
            peer(1)

        @block.vector
        def _(dve):
            v = nc.vector
            st = Steps(dve, dve_done)
            did, need = st.did, st.need
            copy = v.tensor_copy
            dve.sem_inc(u_used, NU)
            dve.sem_inc(w_ready, 4)

            def norm(s, name, gain_no):
                dve.wait_ge(ssq_ready, 2 * s + 2)
                v.tensor_scalar(ms, ssq, 1.0 / D, EPS, ALU.mult, ALU.add).then_inc(ms_ready, 1)
                dve.wait_ge(rstd_ready, s + 1)
                dve.wait_ge(gain_in, 16 * (gain_no + 1))
                for b in range(NB):
                    v.scalar_tensor_tensor(out=xn[b], in0=xb[b], scalar=rstd[:, b:b + 1], in1=gain[:, :],
                                           op0=ALU.mult, op1=ALU.mult).then_inc(xn_ready, 1)
                for g in range(GR[name], GR[name] + 8):
                    if g % 2:
                        copy_group(dve, copy, g, norm_dst(g - GR[name]))

            def add_output(first, layer):
                with dve.Fori(0, 2) as pair:
                    for par in range(2):
                        dve.wait_ge(w_used, pair * 8 + (8 + 4 * (first + par) + 4))
                        for b in range(NB):
                            at = x_sb[:, bass.ds(pair * (2 * CH) + (b * D + par * CH), CH)]
                            v.tensor_tensor(at, acc[2 * par + b][:, :], at, ALU.add).then_inc(acc_out, 1)

            dve.wait_ge(consts_in, 16)
            norm(0, "n0", 0)
            dve.wait_ge(gates_full, 1)
            dve.wait_ge(wg_in, 48)
            n = did(v.tensor_tensor(g_sb[:, :].rearrange("p (b g) -> p b g", b=NB),
                                    mis[0][:, 0:32].rearrange("p (b g) -> p b g", b=NB),
                                    bias[:, :].unsqueeze(1).to_broadcast([P, NB, 16]), ALU.add))
            need(n)
            g4 = g_sb[:, :].rearrange("p (b d t h) -> p (b d) t h", b=NB, d=2, t=2)
            g_i, g_f = g4[:, :, 0, :], g4[:, :, 1, :]

            def w4(t):
                return t[:, 0:16].rearrange("p (x h) -> p x h", h=4)
            v.scalar_tensor_tensor(out=w4(gf), in0=g_f, scalar=-1.0, in1=g_f, op0=ALU.mult, op1=ALU.max).then_inc(exp_in, 1)
            dve.wait_ge(exp_out, 1)
            need(did(v.tensor_scalar(gd[:, 0:16], ge[:, 0:16], 2.0, None, ALU.add)))
            need(did(v.reciprocal(gr[:, 0:16], gd[:, 0:16])))
            need(did(v.tensor_tensor(gz[:, 0:16], ge[:, 0:16], gr[:, 0:16], ALU.mult)))
            need(did(v.tensor_tensor(gz2[:, 0:16], gz[:, 0:16], gz[:, 0:16], ALU.mult)))
            need(did(v.tensor_scalar(gp[:, 0:16], gz2[:, 0:16], 1.0 / 15, None, ALU.mult)))
            for c in (13, 11, 9, 7, 5, 3):
                need(did(v.scalar_tensor_tensor(out=gp[:, 0:16], in0=gp[:, 0:16], scalar=1.0 / c, in1=gz2[:, 0:16],
                                                op0=ALU.add, op1=ALU.mult)))
            need(did(v.scalar_tensor_tensor(out=gp[:, 0:16], in0=gp[:, 0:16], scalar=1.0, in1=gz[:, 0:16],
                                            op0=ALU.add, op1=ALU.mult)))
            need(did(v.tensor_scalar(w4(gd), g_f, 0.0, None, ALU.min)))
            v.scalar_tensor_tensor(out=gls[:, :], in0=gp[:, 0:16], scalar=-2.0, in1=gd[:, 0:16],
                                   op0=ALU.mult, op1=ALU.add).then_inc(ls_ready, 1)
            dve.wait_ge(cum_full, 1)
            did(v.tensor_copy(gB[:, :], mis[1][:, 0:16]))
            v.tensor_tensor(w4(ga), g_i, w4(mis[1]), ALU.subtract).then_inc(a_ready, 1)
            for g in range(8):
                if (GR["qk"] + g) % 2:
                    copy_group(dve, copy, GR["qk"] + g, qkT_dst(g))
            for i in range(8):
                dve.wait_ge(bc_full, i + 1)
                for b in range(NB):
                    mask = shared[:, M_MASK + (2 * (i // 4) + b) * 256:M_MASK + (2 * (i // 4) + b + 1) * 256]
                    v.tensor_tensor_reduce(m_D[:, 2 * i + b, :], mis[i % 2][:, 0:T], mask, 1.0, 0.0, ALU.add,
                                           ALU.max, m_M[:, 2 * i + b:2 * i + b + 1]).then_inc(bc_used, 1)
            dve.wait_ge(bc_used, 16)
            did(v.tensor_scalar(m_negM[:, :], m_M[:, :], -1.0, None, ALU.mult))
            need(st.n)
            v.tensor_tensor(m_nm[:, :].rearrange("p (x b) -> p x b", b=NB),
                            m_negM[:, :].rearrange("p (x b) -> p x b", b=NB),
                            gB[:, :].rearrange("p (b x) -> p x b", b=NB), ALU.subtract).then_inc(negm_ready, 1)
            for i in range(8):
                head, b = i // 2, i % 2
                dve.wait_ge(s_full, i + 1)
                for d in range(2):
                    k = (d * M_HEADS + head) * 2 + b
                    dve.wait_ge(decay_ready, k + 1)
                    v.tensor_tensor_reduce(m_D[:, k, :], mis[i % 2][:, 0:T], m_D[:, k, :], M_QK ** -0.5, 0.0,
                                           ALU.mult, ALU.add, m_den[:, k:k + 1]).then_inc(s_used, 1)
            dve.wait_ge(s_used, 16)
            dve.wait_ge(en_ready, 1)
            need(did(v.scalar_tensor_tensor(out=m_dn[:, :], in0=m_den[:, :], scalar=-1.0, in1=m_den[:, :],
                                            op0=ALU.mult, op1=ALU.max)))
            need(did(v.tensor_tensor(m_dn[:, :], m_dn[:, :], m_en[:, :], ALU.max)))
            need(did(v.reciprocal(m_rr[:, :], m_dn[:, :])))
            for i in range(8):
                did(v.tensor_scalar(m_D[:, i, :], m_D[:, i, :], m_rr[:, i:i + 1], None, ALU.mult))
            for i in range(8):
                need(st.n - 7 + i)
                v.scalar_tensor_tensor(out=m_D[:, i, :], in0=m_D[:, 8 + i, :], scalar=m_rr[:, 8 + i:9 + i],
                                       in1=m_D[:, i, :], op0=ALU.mult, op1=ALU.add).then_inc(p_ready, 1)
            for h in range(M_HEADS):
                if (GR["pt"] + h) % 2:
                    copy_group(dve, copy, GR["pt"] + h, m_PT[:, h, :, :])
            dve.wait_ge(gain_in, 32)
            dve.wait_ge(acc_out, 4 + 24)
            for b in range(NB):
                did(v.tensor_tensor(m_o[:, b, :], m_o[:, b, :], gain[:, :], ALU.mult))
            dve.wait_ge(act_done, 8)
            v.tensor_scalar(h_ms[:, :], h_ssq[:, :], 1.0 / M_V, EPS, ALU.mult, ALU.add).then_inc(msh_ready, 1)
            dve.wait_ge(h_out, 8)
            dve.wait_ge(rh_ready, 1)
            need(st.n)
            for b in range(NB):
                for head in range(M_HEADS):
                    at = m_h[:, b, head * M_V:(head + 1) * M_V]
                    i = 2 * head + b
                    v.scalar_tensor_tensor(out=at, in0=at, scalar=h_r[:, i:i + 1],
                                           in1=m_o[:, b, head * M_V:(head + 1) * M_V],
                                           op0=ALU.mult, op1=ALU.mult).then_inc(h_ready, 1)
            for g in range(8):
                if (GR["h"] + g) % 2:
                    copy_group(dve, copy, GR["h"] + g, norm_dst(g))
            add_output(12, 0)

            def peer(l):
                def topk(gu, su, heads_seen):
                    dve.wait_ge(sc_out, heads_seen)
                    n = did(v.tensor_copy(scur[:, :], scores[:, bass.ds(su * (2 * P), 2 * P)]))
                    need(n)
                    S = [scur[:, i * P:(i + 1) * P] for i in range(2)]
                    R = [srep[:, i * P:(i + 1) * P] for i in range(2)]
                    V8 = [[t_val[:, i * 16 + 8 * r:i * 16 + 8 * r + 8] for r in range(2)] for i in range(2)]
                    I8 = [[t_idx[:, i * 16 + 8 * r:i * 16 + 8 * r + 8] for r in range(2)] for i in range(2)]
                    settle(dve)
                    a = [did(v.max(V8[i][0], S[i])) for i in range(2)]
                    c = []
                    for i in range(2):
                        need(a[i])
                        settle(dve)
                        c.append(did(v.match_replace(R[i], V8[i][0], S[i], -3e38)))
                    for i in range(2):
                        did(v.max_index(I8[i][0], V8[i][0], S[i]))
                    e = []
                    for i in range(2):
                        need(c[i])
                        settle(dve)
                        e.append(did(v.max(V8[i][1], R[i])))
                    for i in range(2):
                        need(e[i])
                        settle(dve)
                        did(v.max_index(I8[i][1], V8[i][1], R[i]))
                    m = st.n
                    n = did(v.tensor_tensor(cand[:, :].rearrange("p (a b) -> p a b", a=16),
                                            t_val[:, 0:16].unsqueeze(2).to_broadcast([P, 16, 16]),
                                            t_val[:, 16:32].unsqueeze(1).to_broadcast([P, 16, 16]), ALU.add))
                    need(st.loop + m)
                    did(v.tensor_copy(t_idf[:, 0:16], t_idx[:, 0:16]))
                    did(v.tensor_scalar(t_idf[:, 16:32], t_idx[:, 16:32], float(l * EXPERTS), None, ALU.add))
                    need(n)
                    settle(dve)
                    need(did(v.max(c_top[:, 0:8], cand[:, :])))
                    did(v.tensor_scalar(negmax[:, :], c_top[:, 0:1], -1.0, None, ALU.mult))
                    n = did(v.match_replace(crep[:, :], c_top[:, 0:8], cand[:, :], -3e38))
                    did(v.max_index(c_pos[:, 0:8], c_top[:, 0:8], cand[:, :]))
                    need(n)
                    settle(dve)
                    v.max(c_top[:, 8:16], crep[:, :]).then_inc(top_ready, 1)
                    dve.wait_ge(top_ready, gu + 1)
                    settle(dve)
                    need(did(v.max_index(c_pos[:, 8:16], c_top[:, 8:16], crep[:, :])))
                    did(v.tensor_scalar(c_ab[:, 0:16], c_pos[:, :], 4, None, ALU.logical_shift_right))
                    need(did(v.tensor_scalar(c_ab[:, 16:32], c_pos[:, :], 15, None, ALU.bitwise_and)))
                    oh = onehot[:, :].rearrange("p (j a) -> p j a", a=16)
                    need(did(v.tensor_tensor(oh, c_ab[:, :].unsqueeze(2).to_broadcast([P, 32, 16]),
                                             iota.unsqueeze(1).to_broadcast([P, 32, 16]), ALU.is_equal)))
                    oh4 = onehot[:, :].rearrange("p (s j a) -> p s j a", s=2, a=16)
                    ids = t_idf[:, :].rearrange("p (s a) -> p s a", s=2).unsqueeze(2).to_broadcast([P, 2, 16, 16])
                    need(did(v.tensor_tensor(oh4, oh4, ids, ALU.mult)))
                    need(did(v.tensor_reduce(sel_if[:, :], oh, AX.X, ALU.add)))
                    if not isinstance(gu, int) or gu > 0:
                        dve.wait_ge(idx_taken, gu)
                    v.scalar_tensor_tensor(out=idx_next[:, :], in0=sel_if[:, 0:16], scalar=float(P),
                                           in1=sel_if[:, 16:32], op0=ALU.mult, op1=ALU.add).then_inc(idx_ready, 1)
                    dve.wait_ge(gexp_ready, gu + 1)
                    need(did(v.reciprocal(g_rec[:, :], g_sum[:, :])))
                    did(v.tensor_scalar(gate_next[:, :], g_exp[:, :], g_rec[:, :], None, ALU.mult))

                def unit(b, gu, nxt):
                    start = st.loop + st.n
                    need(start)
                    dve.wait_ge(w_ready, gu * 4 + 4)
                    did(v.tensor_copy(gate_cur[:, :], gate_next[:, :]))

                    def dot(k):
                        dve.wait_ge(u_landed[k % NU], gu * 64 + (16 * (k // NU) + 16))
                        v.tensor_tensor_reduce(u_slot[k % NU], u_slot[k % NU], xn[b], 1.0, 0.0, ALU.mult, ALU.add,
                                               dots[:, k:k + 1]).then_inc(u_used, 1)

                    def pre(j):
                        c = slice(4 * j, 4 * j + 4)
                        dve.wait_ge(u_used, gu * TOPK + (NU + 4 * j + 4))
                        need(did(v.tensor_tensor(e_x2[:, c], dots[:, c], dots[:, c], ALU.mult)))
                        need(did(v.tensor_scalar(e_t[:, c], e_x2[:, c], GELU_A, 1.0, ALU.mult, ALU.add)))
                        v.tensor_tensor(e_in[:, c], e_t[:, c], dots[:, c], ALU.mult).then_inc(tanh_in, 1)

                    def post(j):
                        c = slice(4 * j, 4 * j + 4)
                        dve.wait_ge(tanh_out, gu * 4 + (j + 1))
                        need(did(v.scalar_tensor_tensor(out=e_p[:, c], in0=e_th[:, c], scalar=1.0, in1=dots[:, c],
                                                        op0=ALU.add, op1=ALU.mult)))
                        v.scalar_tensor_tensor(out=e_w[:, c], in0=e_p[:, c], scalar=0.5, in1=gate_cur[:, c],
                                               op0=ALU.mult, op1=ALU.mult).then_inc(w_ready, 1)

                    for k in range(TOPK):
                        dot(k)
                        if k % 4 == 3:
                            pre(k // 4)
                        if k % 4 == 0 and k:
                            post(k // 4 - 1)
                        if k == 8 and nxt:
                            topk(*nxt)
                    post(3)

                base = l * UNITS
                seen = l * HEADS
                topk(base, 0, seen + 1)
                UNIT_STEPS = 39
                with dve.Fori(0, HEADS - 1) as h:
                    at = st.n
                    st.loop = h * UNIT_STEPS
                    unit(0, h + base, (h + (base + 1), h + 1, h + (seen + 2)))
                    assert st.n - at == UNIT_STEPS, st.n - at
                st.loop = 0
                st.n = at + UNIT_STEPS * (HEADS - 1)
                unit(0, base + HEADS - 1, (base + HEADS, HEADS, seen + HEADS))
                with dve.Fori(0, HEADS - 1) as h:
                    at = st.n
                    st.loop = h * UNIT_STEPS
                    unit(1, h + (base + HEADS), (h + (base + HEADS + 1), h + (HEADS + 1), seen + HEADS))
                    assert st.n - at == UNIT_STEPS, st.n - at
                st.loop = 0
                st.n = at + UNIT_STEPS * (HEADS - 1)
                unit(1, base + UNITS - 1, None)

            norm(1, "n1", 2)
            peer(0)

            norm(2, "n2", 3)
            dve.wait_ge(qkg_in, 32)
            need(did(v.tensor_scalar(qkgain[:, 0:P], qkgain[:, 0:P], DH ** -0.5, None, ALU.mult)))
            HC = CH // DH
            for c in range(5):
                par = c % 2
                dve.wait_ge(sq_ready, 2 * c + 2)
                need(did(v.tensor_reduce(q_ssq[:, :], a_sq.rearrange("p (h d) -> p h d", d=DH), AX.X, ALU.add)))
                v.tensor_scalar(q_ms[:, :], q_ssq[:, :], 1.0 / DH, EPS, ALU.mult, ALU.add).then_inc(msq_ready, 1)
                dve.wait_ge(rq_ready, c + 1)
                g = qkgain[:, 0:P] if c < 4 else qkgain[:, P:2 * P]
                s0 = st.n
                for b in range(NB):
                    v.tensor_tensor(a_y[:, b], acc[2 * par + b][:, :].rearrange("p (h d) -> p h d", d=DH),
                                    q_r[:, b * HC:(b + 1) * HC].unsqueeze(2).to_broadcast([P, HC, DH]),
                                    ALU.mult).then_inc(acc_out, 1)
                for b in range(NB):
                    dve.wait_ge(acc_out, 4 + 2 * (M_CHUNKS + c) + b + 1)
                    did(v.tensor_tensor(a_y[:, b], a_y[:, b], g.unsqueeze(1).to_broadcast([P, HC, DH]), ALU.mult))
                for b in range(NB):
                    need(s0 + 1 + b)
                    cos = const[:, C_COS + b * P:C_COS + (b + 1) * P].unsqueeze(1).to_broadcast([P, HC, DH])
                    sin = const[:, C_SIN + b * 64:C_SIN + (b + 1) * 64].unsqueeze(1).to_broadcast([P, HC, 64])
                    y2 = a_y[:, b].rearrange("p h (e two) -> p h e two", two=2)
                    t2 = a_t2[:, b].rearrange("p h (e two) -> p h e two", two=2)
                    did(v.tensor_tensor(a_t1[:, b], a_y[:, b], cos, ALU.mult))
                    did(v.scalar_tensor_tensor(out=t2[:, :, :, 0], in0=y2[:, :, :, 1], scalar=-1.0, in1=sin,
                                               op0=ALU.mult, op1=ALU.mult))
                    did(v.tensor_tensor(t2[:, :, :, 1], y2[:, :, :, 0], sin, ALU.mult))
                for b in range(NB):
                    need(s0 + 2 + 3 * (b + 1))
                    v.tensor_tensor(aproj[:, b, c * CH:(c + 1) * CH].rearrange("p (h d) -> p h d", d=DH),
                                    a_t1[:, b], a_t2[:, b], ALU.add).then_inc(qk_ready, 1)
            for g in range(2):
                if (GR["akT"] + g) % 2:
                    copy_group(dve, copy, GR["akT"] + g, a_kT[:, 2 * g:2 * g + 2, :])
            for g in range(8):
                if (GR["aqT"] + g) % 2:
                    copy_group(dve, copy, GR["aqT"] + g, actT[:, 2 * g:2 * g + 2, :])
            for h in range(A_HEADS + 1):
                if h < A_HEADS:
                    c = slice(2 * (h % 2), 2 * (h % 2) + 2)
                    dve.wait_ge(as_full, h + 1)
                    need(did(v.tensor_reduce(a_mx[:, c], mis[h % 2][:, :].rearrange("p (b s) -> p b s", b=NB),
                                             AX.X, ALU.max)))
                    v.tensor_scalar(a_nmx[:, c], a_mx[:, c], -1.0, None, ALU.mult).then_inc(amax_ready, 1)
                    dve.wait_ge(ap_ready, 2 * h + 2)
                    need(did(v.reciprocal(a_rs[:, c], a_sum[:, c])))
                    for b in range(NB):
                        v.tensor_scalar(a_P[h % 2][:, b, :], a_P[h % 2][:, b, :],
                                        a_rs[:, 2 * (h % 2) + b:2 * (h % 2) + b + 1], None, ALU.mult).then_inc(an_ready, 1)
                if h >= 1 and (GR["apt"] + h - 1) % 2:
                    if h >= 3:
                        dve.wait_ge(o_full, h - 2)
                    copy_group(dve, copy, GR["apt"] + h - 1, a_PT[(h - 1) % 2])
            add_output(22, 1)
            norm(3, "n3", 4)
            peer(1)


_INS = ["x", "ln_mix", "ln_ffn", "mlstm_w_in", "mlstm_gate_bias", "mlstm_head_norm", "mlstm_w_out", "attn_w_in",
        "attn_q_norm", "attn_k_norm", "attn_w_out", "peer_wq", "peer_k1", "peer_k2", "peer_u", "peer_v"]


def kernel(**inputs):
    import numpy as _np
    import concourse.bacc as _bacc
    from concourse import mybir as _mybir
    from concourse.bass_utils import run_bass_kernel_spmd as _run

    nc = _bacc.Bacc("TRN2", target_bir_lowering=False, num_devices=1)
    arrays, args = {}, []
    for name in ["consts"] + _INS:
        if name == "consts":
            a = constants()
        else:
            a = _np.asarray(inputs[name])
            if name in ("peer_k1", "peer_k2"):
                a = a.transpose(0, 2, 1)
            a = _np.ascontiguousarray(a)
        arrays[f"in_{name}_dram"] = a
        args.append(nc.dram_tensor(f"in_{name}_dram", a.shape, _mybir.dt.from_np(a.dtype), kind="ExternalInput").ap())
    shape = _np.asarray(inputs["x"]).shape
    args.append(nc.dram_tensor("out_dram", shape, _mybir.dt.float32, kind="ExternalOutput").ap())
    trunk_kernel(nc, *args)
    r = _run(nc, [arrays], core_ids=[0])
    return r.results[0]["out_dram"]
```

```python
import concourse.bass as bass
from concourse import mybir
from contextlib import ExitStack
import numpy as np

F32 = mybir.dt.float32
F32R = mybir.dt.float32r
U32 = mybir.dt.uint32
ALU = mybir.AluOpType
ACT = mybir.ActivationFunctionType
AX = mybir.AxisListType

P = 128
GRID_W = 64
EPS = 1e-6
ROPE_THETA = 10000.0
MASKED = -1e30
GELU_C = float(np.sqrt(2.0 / np.pi))
GELU_A = 0.044715

C_ID, C_IOTA, C_POW = 0, 128, 144
C_COS = C_POW + 8
C_SIN = C_COS + 256
C_KEPT = C_SIN + 128
M_TRI, M_ONES, M_MASK = 0, 256, 384
M_SEL = M_MASK + 4 * 256
M_ALL = M_SEL + 8 * 128
C_TRI, C_ONES, C_MASK, C_SEL = (C_KEPT + m for m in (M_TRI, M_ONES, M_MASK, M_SEL))
C_ALL = C_KEPT + M_ALL


def constants():
    c = np.zeros((P, C_ALL), np.float32)
    r = np.arange(P)
    c[:, C_ID:C_ID + P] = np.eye(P)
    c[:, C_TRI:C_TRI + P] = r[:, None] <= r[None, :]
    c[:, C_TRI + P:C_TRI + 2 * P] = r[:, None] >= r[None, :]
    c[:, C_ONES:C_ONES + P] = 1.0
    s = np.arange(2 * P)
    for d in range(2):
        for b in range(2):
            t = (b * P + r)[:, None]
            seen = (s[None, :] <= t) if d == 0 else (s[None, :] >= t)
            at = C_MASK + (2 * d + b) * 256
            c[:, at:at + 256] = np.where(seen, 0.0, MASKED)
    c[:, C_IOTA:C_IOTA + 16] = np.arange(16)
    n_freq = P // 4
    freqs = (np.float32(ROPE_THETA) ** (-np.arange(n_freq, dtype=np.float32) / np.float32(n_freq))).astype(np.float32)
    for b in range(2):
        t = b * P + r
        row, col = (t // GRID_W).astype(np.float32), (t % GRID_W).astype(np.float32)
        ang = np.concatenate([row[:, None] * freqs, col[:, None] * freqs], axis=-1).astype(np.float32)
        c[:, C_COS + b * P:C_COS + (b + 1) * P] = np.repeat(np.cos(ang), 2, axis=-1)
        c[:, C_SIN + b * 64:C_SIN + (b + 1) * 64] = np.sin(ang)
    for i in range(8):
        c[i, C_SEL + i * P:C_SEL + (i + 1) * P] = 1.0
    c[:, C_POW:C_POW + 8] = -0.5
    return c


class Steps:

    def __init__(self, eng, sem):
        self.eng, self.sem, self.n, self.loop = eng, sem, 0, 0

    def did(self, ins):
        self.n += 1
        ins.then_inc(self.sem, 1)
        return self.loop + self.n

    def need(self, count):
        self.eng.wait_ge(self.sem, count)


def trunk_kernel(nc, consts, x, ln_mix, ln_ffn, m_w_in, m_gate_bias, m_head_norm, m_w_out,
                 a_w_in, a_q_norm, a_k_norm, a_w_out, wq, k1T, k2T, u_tab, v_tab, out):
    D = x.shape[-1]
    KT = D // P
    NB = x.shape[1] // P
    T = NB * P
    M_HEADS, M_V = m_head_norm.shape[1:]
    M_QK = M_V // 2
    NQK, NV = M_HEADS * M_QK, M_HEADS * M_V
    DH = a_q_norm.shape[-1]
    A_HEADS = a_w_out.shape[1] // DH
    A_KV = (a_w_in.shape[2] // DH - A_HEADS) // 2
    HEADS = wq.shape[2] // (2 * P)
    TOPK = 16
    CH = 512
    QK = KT // 4
    SLOT = QK * CH
    NU, NVS = 4, 8
    UNITS = NB * HEADS
    assert SLOT == D and NB == 2 and T == 256 and M_V == CH and DH == P

    with ExitStack() as ctx:
        def sb(name, cols, dt=F32, rows=P):
            return ctx.enter_context(nc.sbuf_tensor(name, [rows, cols], dt))

        placed = {}

        def sb_placed(name, cols):
            placed[name] = -(-nc.sbuf_base // 32) * 32
            return sb(name, cols)

        def parts_in(name, cols, host, at=0):
            return nc.alloc_sbuf_tensor_at(name, [P, cols], F32R, offset=placed[host] + 4 * at)

        def sem(name):
            return ctx.enter_context(nc.semaphore(name))

        const = sb("const", C_KEPT)
        shared = sb("shared", 3072)
        x_sb = sb("x_sb", NB * D)
        actT_sb = sb_placed("actT_sb", KT * T)
        ring_sb = sb_placed("ring_sb", (NU + NVS) * SLOT)
        arena = sb("arena", 3 * NB * D)
        gain = sb("gain", D)
        w_gate = sb("w_gate", KT * 16)
        bias = sb("bias", 16)
        small = sb("small", 40)
        keysT = sb("keysT", 2 * P)
        qkgain = sb("qkgain", 2 * P)

        ident = const[:, C_ID:C_ID + P]
        tri = [shared[:, M_TRI + d * P:M_TRI + (d + 1) * P] for d in range(2)]
        ones = shared[:, M_ONES:M_ONES + P]
        iota = const[:, C_IOTA:C_IOTA + 16]
        xb = [x_sb[:, b * D:(b + 1) * D] for b in range(NB)]
        actT = actT_sb[:, :].rearrange("p (k t) -> p k t", t=T)
        ring = [ring_sb[:, s * SLOT:(s + 1) * SLOT] for s in range(NU + NVS)]
        w_parts = parts_in("w_parts", 8 * SLOT, "ring_sb")
        w_lo_of = [w_parts[:, j * SLOT:(j + 1) * SLOT] for j in range(4)]
        w_hi_of = [w_parts[:, (4 + j) * SLOT:(5 + j) * SLOT] for j in range(4)]
        actT_hi = parts_in("actT_hi", KT * T, "actT_sb")[:, :].rearrange("p (k t) -> p k t", t=T)
        actT_lo = parts_in("actT_lo", KT * T, "ring_sb", 10 * SLOT)[:, :].rearrange("p (k t) -> p k t", t=T)
        w_gate_parts = parts_in("w_gate_parts", 2 * KT * 16, "ring_sb", 9 * SLOT)
        w_gate_hi, w_gate_lo = (w_gate_parts[:, i * KT * 16:(i + 1) * KT * 16] for i in range(2))
        gatesT = ring[8][0:16, 0:T]
        xn = [arena[:, b * D:(b + 1) * D] for b in range(NB)]
        ssq, ms, rstd = small[:, 0:2], small[:, 8:10], small[:, 16:18]

        EXPERTS = u_tab.shape[1]
        u_rows, v_rows = (t.rearrange("l e d -> (l e) d") for t in (u_tab, v_tab))

        banks = [ctx.enter_context(nc.psum_tensor(f"bank{i}", [P, CH], F32)) for i in range(8)]
        acc, trb, mis = banks[0:4], banks[4:6], banks[6:8]

        consts_in, shared_in, gain_in = sem("consts_in"), sem("shared_in"), sem("gain_in")
        x_in = [sem("x_in0"), sem("x_in1")]
        keys_in, wg_in, qkg_in = sem("keys_in"), sem("wg_in"), sem("qkg_in")
        dve_done, act_done = sem("dve_done"), sem("act_done")
        ssq_ready, ms_ready, rstd_ready, xn_ready = sem("ssq_ready"), sem("ms_ready"), sem("rstd_ready"), sem("xn_ready")
        tr_full = [sem("tr_full_act"), sem("tr_full_dve")]
        tr_out = [sem("tr_out_act"), sem("tr_out_dve")]
        tr_hi = sem("tr_hi")
        w_landed = [sem(f"w_landed{j}") for j in range(4)]
        w_hi = sem("w_hi")
        w_lo = [sem(f"w_lo{j}") for j in range(4)]
        w_used = sem("w_used")
        first_full = sem("first_full")
        acc_out = sem("acc_out")
        wg_hi, wg_lo, gT_full, gT_ready = sem("wg_hi"), sem("wg_lo"), sem("gT_full"), sem("gT_ready")
        gates_full, exp_in, exp_out, ls_ready, cum_full = (sem(n) for n in ("gates_full", "exp_in", "exp_out", "ls_ready", "cum_full"))
        a_ready, bc_full, bc_used = sem("a_ready"), sem("bc_full"), sem("bc_used")
        negm_ready, en_ready, decay_ready = sem("negm_ready"), sem("en_ready"), sem("decay_ready")
        s_full, s_used, p_ready = sem("s_full"), sem("s_used"), sem("p_ready")
        h_full, h_out, msh_ready, rh_ready, h_ready = (sem(n) for n in ("h_full", "h_out", "msh_ready", "rh_ready", "h_ready"))
        sq_ready, msq_ready, rq_ready, qk_ready = (sem(n) for n in ("sq_ready", "msq_ready", "rq_ready", "qk_ready"))
        as_full, amax_ready, ap_ready, an_ready, o_full, o_hi, o_out = (sem(n) for n in ("as_full", "amax_ready", "ap_ready", "an_ready", "o_full", "o_hi", "o_out"))
        wq_landed = [sem("wq_landed0"), sem("wq_landed1")]
        wq0_landed = [sem("wq0_landed0"), sem("wq0_landed1")]
        rq_full, rq_out, rt_full, rt_out, sc_full, sc_out = (sem(n) for n in ("rq_full", "rq_out", "rt_full", "rt_out", "sc_full", "sc_out"))
        top_ready, gexp_ready, idx_ready, idx_taken = (sem(n) for n in ("top_ready", "gexp_ready", "idx_ready", "idx_taken"))
        u_landed = [sem(f"u_landed{s}") for s in range(NU)]
        v_landed = [sem(f"v_landed{s}") for s in range(NVS)]
        u_used = sem("u_used")
        v_used = sem("v_used")
        tanh_in, tanh_out, w_ready, diag_ready = sem("tanh_in"), sem("tanh_out"), sem("w_ready"), sem("diag_ready")
        x_out, stored = sem("x_out"), sem("stored")

        mproj = arena[:, :].rearrange("p (b n) -> p b n", b=NB)
        m_v = mproj[:, :, 2 * NQK:2 * NQK + NV]
        m_o = mproj[:, :, 2 * NQK + NV:2 * NQK + 2 * NV]
        m_h = mproj[:, :, 0:NV]
        m_qkT = ring_sb[:, 8 * SLOT:10 * SLOT].rearrange("p (k t) -> p k t", t=T)

        def m_D(u):
            return mproj[:, u // 8, (u % 8) * T:(u % 8 + 1) * T]

        m_PT = actT_sb[:, 0:M_HEADS * 2 * T].rearrange("p (h s t) -> p h s t", h=M_HEADS, s=NB)
        g_sb, gf, ge, gd, gr, gz, gz2, gp = (sb(f"gate{i}", 32) for i in range(8))
        gls, ga, gB = sb("gls", 16), sb("ga", 16), sb("gB", 16)
        aT = sb("aT", T, rows=8)
        m_M, m_negM, m_nm, m_en, m_den, m_dn, m_rr = (sb(f"m_stat{i}", 16) for i in range(7))
        h_ssq, h_ms, h_r = sb("h_ssq", 8), sb("h_ms", 8), sb("h_r", 8)
        h_junk = ring[8][:, 0:CH]

        aproj = arena[:, 0:NB * 3072].rearrange("p (b n) -> p b n", b=NB)
        a_sq = arena[:, 6144:7168]
        a_y = arena[:, 7168:8192].rearrange("p (b h d) -> p b h d", b=NB, d=DH)
        a_t1 = arena[:, 8192:9216].rearrange("p (b h d) -> p b h d", b=NB, d=DH)
        a_t2 = arena[:, 9216:10240].rearrange("p (b h d) -> p b h d", b=NB, d=DH)
        a_kT = ring[8][:, 0:A_KV * T].rearrange("p (k t) -> p k t", t=T)
        a_P = [ring[9][:, i * 512:(i + 1) * 512].rearrange("p (b s) -> p b s", b=NB) for i in range(2)]
        a_PT = [ring[9][:, 1024 + i * 512:1024 + (i + 1) * 512].rearrange("p (s t) -> p s t", s=NB) for i in range(2)]
        a_mx, a_nmx, a_sum, a_rs = (sb(f"a_stat{i}", 4) for i in range(4))
        q_ssq, q_ms, q_r = sb("q_ssq", 8), sb("q_ms", 8), sb("q_r", 8)

        scores = arena[:, 2 * D:4 * D]
        scores_bh = scores.rearrange("p (b r) -> p b r", b=NB)
        wq_slot = [arena[:, (4 + i) * D:(5 + i) * D].rearrange("p (k n) -> p k n", n=2 * P) for i in range(2)]
        taken = [0]

        def tile(cols, dt=F32):
            taken[0] += cols
            assert taken[0] <= 3072
            t = shared[:, taken[0] - cols:taken[0]]
            return t.bitcast(dt) if dt is not F32 else t

        q_nat, q_T, onehot = tile(2 * 2 * P), tile(2 * 2 * P), tile(512)
        scur, srep, cand, crep = tile(2 * P), tile(2 * P), tile(256), tile(256)
        t_val, t_idx, t_idf = tile(32), tile(32, U32), tile(32)
        c_top, c_pos, c_ab, sel_if = tile(16), tile(16, U32), tile(32, U32), tile(32)
        negmax, g_exp, g_sum, g_rec, gate_next, gate_cur = tile(1), tile(16), tile(1), tile(1), tile(16), tile(16)
        idx_next = sb("idx_next", 16, U32)
        idx_cur = [sb("idx_cur0", 16, U32), sb("idx_cur1", 16, U32)]
        dots, e_x2, e_t, e_in, e_th, e_p, e_w = (tile(16) for i in range(7))
        diag = [sb(f"diag{i}", P) for i in range(4)]
        u_slot, v_slot = ring[0:NU], ring[NU:NU + NVS]
        FIRST_QUERY_SLOT = 4
        wq0_slot = [v_slot[FIRST_QUERY_SLOT + i].rearrange("p (k n) -> p k n", n=2 * P) for i in range(2)]

        GR = {}
        n_groups = 0
        for name, n in (("n0", 8), ("qk", 8), ("a", 1), ("pt", M_HEADS), ("h", 8), ("n1", 8), ("n2", 8),
                        ("akT", 2), ("aqT", 8), ("apt", A_HEADS), ("n3", 8)):
            GR[name] = n_groups
            n_groups += n

        def wait_bank(pe, g):
            if g >= 2:
                pe.wait_ge(tr_out[g % 2], g // 2)

        def wait_groups(eng, first, n):
            for par in range(2):
                last = max((g for g in range(first, first + n) if g % 2 == par), default=None)
                if last is not None:
                    eng.wait_ge(tr_out[par], last // 2 + 1)

        def copy_group(eng, copy, g, dst, cols=512, rows=P):
            eng.wait_ge(tr_full[g % 2], g // 2 + 1)
            src = trb[g % 2][0:rows, 0:cols]
            if len(dst.shape) == 3:
                src = src.rearrange("p (k t) -> p k t", t=dst.shape[2])
            copy(dst, src).then_inc(tr_out[g % 2], 1)

        def norm_dst(g, of=None):
            b, q = g // 4, g % 4
            return (actT if of is None else of)[:, 4 * q:4 * q + 4, b * P:(b + 1) * P]

        SPLIT = {name: 8 * i for i, name in enumerate(("n0", "h", "n2"))}

        def hi_groups(act, copy, name, groups):
            for g in groups:
                at = GR[name] + g
                act.wait_ge(tr_full[at % 2], at // 2 + 1)
                copy(norm_dst(g, actT_hi), trb[at % 2][:, :].rearrange("p (k t) -> p k t", t=P)).then_inc(tr_hi, 1)

        def lo_groups(dve, name, groups):
            for g in groups:
                at = GR[name] + g
                dve.wait_ge(tr_hi, SPLIT[name] + g + 1)
                nc.vector.tensor_tensor(norm_dst(g, actT_lo), trb[at % 2][:, :].rearrange("p (k t) -> p k t", t=P),
                                        norm_dst(g, actT_hi).bitcast(F32), ALU.subtract).then_inc(tr_out[at % 2], 1)

        def hi_weights(act, c, quarters):
            for j in quarters:
                act.wait_ge(w_landed[j], c * 16 + 16)
                nc.scalar.copy(w_hi_of[j], ring[j]).then_inc(w_hi, 1)

        def lo_weights(eng, ops, c, quarters):
            for j in quarters:
                eng.wait_ge(w_hi, c * 4 + (j + 1))
                ops.tensor_tensor(w_lo_of[j], ring[j], w_hi_of[j].bitcast(F32), ALU.subtract).then_inc(w_lo[j], 1)

        def qkT_dst(g):
            return m_qkT[:, 2 * g:2 * g + 2, :]

        GROUPS = [(k, k + 4) for k in range(0, TOPK, 4)]
        LAST_GROUPS = GROUPS[:2] + [(k, k + 1) for k in range(8, TOPK)]
        EXTRA = len(LAST_GROUPS) - len(GROUPS)

        W_CH = {"m_in": (0, 12), "m_out": (12, 4), "a_in": (16, 6), "a_out": (22, 4)}
        M_CHUNKS = 16
        ALL_CHUNKS = 26

        waits_passed = {"pool": sem("pool_waits_passed"), "dve": sem("dve_waits_passed")}

        def settle(eng):
            eng.sem_inc(waits_passed["pool" if eng is pool_engine[0] else "dve"], 1)

        pool_engine = [None]
        block = ctx.enter_context(nc.Block())

        @block.sync
        def _(sp):
            sp.dma_start(xb[0], x[0, 0:P, :]).then_inc(x_in[0], 16)
            sp.dma_start(const[:, :], consts[:, 0:C_KEPT]).then_inc(consts_in, 16)
            sp.dma_start(gain[:, :], ln_mix[0].partition_broadcast(P)).then_inc(gain_in, 16)
            sp.dma_start(xb[1], x[0, P:2 * P, :]).then_inc(x_in[1], 16)
            sp.dma_start(w_gate[:, :].rearrange("p (k n) -> p k n", n=16),
                         m_w_in[0, :, 2 * NQK + 2 * NV:].rearrange("(k p) n -> p k n", p=P)).then_inc(wg_in, 16)
            sp.dma_start(bias[:, :], m_gate_bias[0].rearrange("t h -> (t h)").partition_broadcast(P)).then_inc(wg_in, 16)

            def load_chunks(w, first, n):
                with sp.Fori(0, n) as c:
                    for j in range(4):
                        sp.wait_ge(w_used, c * 4 + (4 * first + j + 1))
                        src = w[j * CH:(j + 1) * CH, bass.ds(c * CH, CH)]
                        sp.dma_start(ring[j].rearrange("p (k n) -> p k n", n=CH),
                                     src.rearrange("(k p) n -> p k n", p=P)).then_inc(w_landed[j], 16)

            def load_queries(l):
                keys = [k1T, k2T]
                for i in range(2):
                    if l:
                        sp.wait_ge(sc_out, HEADS + 1)
                    sp.dma_start(keysT[:, i * P:(i + 1) * P], keys[i][l]).then_inc(keys_in, 16)
                half = D // 2

                def load(h, slots=wq_slot, landed=wq_landed):
                    for i in range(2):
                        sp.dma_start(slots[i], wq[l, i * half:(i + 1) * half, bass.ds(h * (2 * P), 2 * P)]
                                     .rearrange("(k p) n -> p k n", p=P)).then_inc(landed[i], 16)
                load(0, wq0_slot, wq0_landed)
                load(1)
                with sp.Fori(2, HEADS) as h:
                    sp.wait_ge(rq_full, h + (l * (HEADS + 1) + 1))
                    load(h)

            load_chunks(m_w_in[0], *W_CH["m_in"])
            load_chunks(m_w_out[0], *W_CH["m_out"])
            sp.wait_ge(h_ready, 8)
            load_queries(0)
            for i, g in enumerate((a_q_norm, a_k_norm)):
                sp.dma_start(qkgain[:, i * P:(i + 1) * P], g[0].partition_broadcast(P)).then_inc(qkg_in, 16)
            sp.wait_ge(u_used, NU + UNITS * TOPK)
            load_chunks(a_w_in[0], *W_CH["a_in"])
            load_chunks(a_w_out[0], *W_CH["a_out"])
            sp.wait_ge(o_full, A_HEADS)
            load_queries(1)
            sp.wait_ge(x_out, 4 * (NB + 1))
            sp.dma_start(out[0, 0:P, :], xb[0]).then_inc(stored, 16)
            for n in range(4):
                sp.wait_ge(x_out, 4 * (NB + 1) + n + 1)
                sp.dma_start(out[0, P:2 * P, n * CH:(n + 1) * CH], xb[1][:, n * CH:(n + 1) * CH]).then_inc(stored, 16)
            sp.wait_ge(stored, 16 * 5)

        @block.gpsimd
        def _(pool):
            pool_engine[0] = pool
            pool.wait_ge(consts_in, 16)
            minus_half = const[:, C_POW:C_POW + 8]

            def rsqrt_of(out_, in_, n):
                return nc.gpsimd.tensor_tensor(out_, in_, minus_half[:, 0:n], ALU.pow)

            def norm(s, blocks=range(NB)):
                for b in blocks:
                    pool.wait_ge(ms_ready, 2 * s + b + 1)
                    rsqrt_of(rstd[:, b:b + 1], ms[:, b:b + 1], 1).then_inc(rstd_ready, 1)

            def gathers(l):
                pool.wait_ge(w_used, 4 + 4 * (M_CHUNKS if l == 0 else ALL_CHUNKS))
                if l:
                    pool.wait_ge(acc_out, 4 + 2 * ALL_CHUNKS)

                def unit(gu, par, first=False):
                    pool.wait_ge(idx_ready, gu + 1)
                    settle(pool)
                    nc.gpsimd.tensor_copy(idx_cur[par][:, :], idx_next[:, :]).then_inc(idx_taken, 1)
                    pool.wait_ge(idx_taken, gu + 1)
                    for k in range(TOPK):
                        pool.wait_ge(u_used, gu * TOPK + (k + 1))
                        settle(pool)
                        nc.gpsimd.indirect_dma_start(
                            out=u_slot[k % NU], out_offset=None, in_=u_rows,
                            in_offset=bass.IndirectOffsetOnAxis(ap=idx_cur[par][:, k:k + 1], axis=0),
                        ).then_inc(u_landed[k % NU], 16)
                        if first and k == FIRST_QUERY_SLOT:
                            pool.wait_ge(rq_full, l * (HEADS + 1) + 2)
                        pool.wait_ge(v_used, gu * TOPK + (k + 1))
                        settle(pool)
                        nc.gpsimd.indirect_dma_start(
                            out=v_slot[k % NVS], out_offset=None, in_=v_rows,
                            in_offset=bass.IndirectOffsetOnAxis(ap=idx_cur[par][:, k:k + 1], axis=0),
                        ).then_inc(v_landed[k % NVS], 16)
                        if first and k == 0:
                            norm(2 * l + 1, [1])

                for par in range(2):
                    unit(l * UNITS + par, par, par == 0)
                with pool.Fori(1, UNITS // 2) as pair:
                    for par in range(2):
                        unit(pair * 2 + (l * UNITS + par), par)

            def lo_chunks(first, end):
                with pool.Fori(first, end) as c:
                    lo_weights(pool, nc.gpsimd, c, range(4))

            norm(0)
            lo_chunks(1, 13)
            for b in range(NB):
                pool.wait_ge(msh_ready, b + 1)
                rsqrt_of(h_r[:, 4 * b:4 * b + 4], h_ms[:, 4 * b:4 * b + 4], 4).then_inc(rh_ready, 1)
            lo_chunks(13, 16)
            norm(1, [0])
            gathers(0)
            norm(2)
            lo_weights(pool, nc.gpsimd, 16, [2, 3])
            lo_weights(pool, nc.gpsimd, 17, range(3))
            for c in range(5):
                pool.wait_ge(msq_ready, c + 1)
                rsqrt_of(q_r[:, :], q_ms[:, :], 8).then_inc(rq_ready, 1)
                lo_weights(pool, nc.gpsimd, 17 + c, [3])
                lo_weights(pool, nc.gpsimd, 18 + c, range(3))
            lo_weights(pool, nc.gpsimd, 22, [3])
            lo_chunks(23, 26)
            norm(3, [0])
            gathers(1)

        @block.scalar
        def _(act):
            st = Steps(act, act_done)
            copy = nc.scalar.copy
            act.sem_inc(acc_out, 4)
            gains = [ln_mix[0], m_head_norm[0].rearrange("h v -> (h v)"), ln_ffn[0], ln_mix[1], ln_ffn[1]]

            def load_gain(i):
                act.dma_start(gain[:, :], gains[i].partition_broadcast(P)).then_inc(gain_in, 16)

            def square(s, b):
                if s == 0:
                    act.wait_ge(x_in[b], 16)
                elif s % 2 == 1:
                    act.wait_ge(acc_out, 4 + 2 * (M_CHUNKS if s == 1 else ALL_CHUNKS) - 1 + b)
                else:
                    act.wait_ge(x_out, 4 * (NB * (s // 2 - 1) + b + 1))
                nc.scalar.activation(xn[b], xb[b], ACT.Square, accum_out=ssq[:, b:b + 1]).then_inc(ssq_ready, 1)

            def copy_groups(name, b, dst):
                for g in range(4 * b, 4 * b + 4):
                    if (GR[name] + g) % 2 == 0:
                        copy_group(act, copy, GR[name] + g, dst(g))

            def split_ahead(c, quarters=3):
                hi_weights(act, c, [3])
                hi_weights(act, c + 1, range(quarters))

            def project_chunk(dst, pair, par, func=ACT.Copy):
                c = pair * 2 + par
                split_ahead(c)
                for b in range(NB):
                    if b == 0:
                        act.wait_ge(first_full, c + 1)
                    else:
                        act.wait_ge(w_used, c * 4 + 8)
                    nc.scalar.activation(dst[:, b, bass.ds(pair * (2 * CH) + par * CH, CH)],
                                         acc[2 * par + b][:, :], func).then_inc(acc_out, 1)

            def project(dst, c0, c1, func=ACT.Copy):
                with act.Fori(c0 // 2, c1 // 2) as pair:
                    for par in range(2):
                        project_chunk(dst, pair, par, func)

            for b in range(NB):
                square(0, b)
            act.dma_start(shared[:, 0:M_ALL], consts[:, C_KEPT:C_ALL]).then_inc(shared_in, 16)
            hi_groups(act, copy, "n0", range(8))
            hi_weights(act, 0, range(3))
            act.wait_ge(xn_ready, 2)
            load_gain(1)
            act.wait_ge(wg_in, 32)
            copy(w_gate_hi[:, :], w_gate[:, :]).then_inc(wg_hi, 1)
            project(mproj, 0, 2)
            act.wait_ge(exp_in, 1)
            nc.scalar.activation(ge[:, 0:16], gf[:, 0:16], ACT.Exp, scale=-1.0).then_inc(exp_out, 1)
            project(mproj, 2, 4)
            for g in range(8):
                if (GR["qk"] + g) % 2 == 0:
                    copy_group(act, copy, GR["qk"] + g, qkT_dst(g))
            project(mproj, 4, 6)
            copy_group(act, copy, GR["a"], aT[:, :], cols=T, rows=8)
            project_chunk(mproj, 3, 0)
            act.wait_ge(negm_ready, 1)
            nc.scalar.activation(m_en[:, :], m_nm[:, :], ACT.Exp).then_inc(en_ready, 1)
            for i in range(16):
                nc.scalar.activation(m_D(i), m_D(i), ACT.Exp,
                                     bias=m_negM[:, i:i + 1]).then_inc(decay_ready, 1)
            project_chunk(mproj, 3, 1)
            project(mproj, 8, 12, ACT.Sigmoid)
            for h in range(M_HEADS):
                if (GR["pt"] + h) % 2 == 0:
                    copy_group(act, copy, GR["pt"] + h, m_PT[:, h, :, :])
            for i in range(8):
                act.wait_ge(h_full, i + 1)
                b, head = i // 4, i % 4
                nc.scalar.copy(m_h[:, b, head * M_V:(head + 1) * M_V], acc[i % 4][:, :]).then_inc(h_out, 1)
                if i:
                    st.need(st.n)
                st.did(nc.scalar.activation(h_junk, acc[i % 4][:, :], ACT.Square, accum_out=h_ssq[:, i:i + 1]))
                if i == 3:
                    hi_weights(act, 12, [3])
            hi_groups(act, copy, "h", range(8))
            hi_weights(act, 13, range(3))
            with act.Fori(13, 15) as c:
                split_ahead(c)
            hi_weights(act, 15, [3])

            def peer(l):
                def router(h, blocks=slice(0, NB)):
                    n = h + (l * (HEADS + 1) + 1) if blocks != slice(0, 1) else l * (HEADS + 1)
                    lo, hi = blocks.start, blocks.stop
                    act.wait_ge(rq_full, n + 1)
                    nc.scalar.copy(q_nat[:, lo * 2 * P:hi * 2 * P], mis[0][:, lo * 2 * P:hi * 2 * P]).then_inc(rq_out, 1)
                    act.wait_ge(rt_full, n + 1)
                    q_t = [t.rearrange("p (s t) -> p s t", s=2)[:, :, lo * P:hi * P] for t in (q_T[:, :], trb[0][:, :])]
                    nc.scalar.copy(*q_t).then_inc(rt_out, 1)
                    act.wait_ge(sc_full, n + 1)
                    nc.scalar.copy(scores_bh[:, blocks, bass.ds(h * (2 * P), 2 * P)],
                                   mis[1][:, lo * 2 * P:hi * 2 * P].rearrange("p (b n) -> p b n", b=hi - lo)).then_inc(sc_out, 1)

                def gate_exp(gu):
                    act.wait_ge(top_ready, gu + 1)
                    nc.scalar.activation(g_exp[:, :], c_top[:, :], ACT.Exp, bias=negmax[:, :],
                                         accum_out=g_sum[:, :]).then_inc(gexp_ready, 1)

                def unit(gu, more, groups=GROUPS, head=None):
                    for j, (k0, k1) in enumerate(groups):
                        if j == 1 and head is not None:
                            router(head)
                        act.wait_ge(tanh_in, gu * 4 + (EXTRA * l + j + 1))
                        nc.scalar.activation(e_th[:, k0:k1], e_in[:, k0:k1], ACT.Tanh, scale=GELU_C).then_inc(tanh_out, 1)
                        act.wait_ge(w_ready, gu * 4 + (EXTRA * l + j + 5))
                        for k in range(k0, k1):
                            act.wait_ge(v_used, gu * TOPK + (k - 4 + NVS + 1))
                            nc.scalar.activation(diag[k % 4][:, :], ident, ACT.Copy,
                                                 scale=e_w[:, k:k + 1]).then_inc(diag_ready, 1)
                        if j == 1 and more:
                            gate_exp(gu + 1)

                def results(b):
                    act.wait_ge(v_used, NVS + (l * UNITS + (b + 1) * HEADS) * TOPK)
                    for n in range(4):
                        nc.scalar.copy(xb[b][:, n * CH:(n + 1) * CH], acc[n][:, :]).then_inc(x_out, 1)

                base = l * UNITS
                name = f"n{2 * l + 1}"
                square(2 * l + 1, 0)
                copy_groups(name, 0, norm_dst)
                router(0, slice(0, 1))
                gate_exp(base)
                square(2 * l + 1, 1)
                copy_groups(name, 1, norm_dst)
                router(0, slice(1, 2))
                if l == 0:
                    act.wait_ge(xn_ready, 4)
                    load_gain(3)
                with act.Fori(0, HEADS - 1) as h:
                    unit(h + base, True, head=h + 1)
                unit(base + HEADS - 1, True)
                results(0)
                if l == 0:
                    square(2, 0)
                with act.Fori(0, HEADS - 1) as h:
                    unit(h + (base + HEADS), True)
                unit(base + UNITS - 1, False, LAST_GROUPS)
                results(1)

            act.wait_ge(h_ready, 8)
            load_gain(2)
            peer(0)

            hi_weights(act, 16, [0])
            hi_groups(act, copy, "n2", range(0, 4))
            square(2, 1)
            hi_weights(act, 16, [1, 2])
            hi_groups(act, copy, "n2", range(4, 8))
            hi_weights(act, 16, [3])
            act.wait_ge(xn_ready, 6)
            load_gain(4)
            for c in range(5):
                par = c % 2
                if c:
                    hi_weights(act, 16 + c, [3])
                hi_weights(act, 17 + c, range(3))
                if c:
                    act.wait_ge(msq_ready, c)
                for b in range(NB):
                    if b == 0:
                        act.wait_ge(first_full, W_CH["a_in"][0] + c + 1)
                    else:
                        act.wait_ge(w_used, 4 + 4 * (W_CH["a_in"][0] + c) + 4)
                    nc.scalar.activation(a_sq[:, b * CH:(b + 1) * CH], acc[2 * par + b][:, :],
                                         ACT.Square).then_inc(sq_ready, 1)
            split_ahead(21)
            act.wait_ge(w_used, 4 + 4 * (W_CH["a_in"][0] + 5) + 4)
            act.wait_ge(acc_out, 4 + 2 * (M_CHUNKS + 5))
            for b in range(NB):
                nc.scalar.copy(aproj[:, b, 5 * CH:6 * CH], acc[2 + b][:, :]).then_inc(acc_out, 1)
            for g in range(2):
                if (GR["akT"] + g) % 2 == 0:
                    copy_group(act, copy, GR["akT"] + g, a_kT[:, 2 * g:2 * g + 2, :])
            for g in range(8):
                if (GR["aqT"] + g) % 2 == 0:
                    copy_group(act, copy, GR["aqT"] + g, actT[:, 2 * g:2 * g + 2, :])
            hi_weights(act, 22, [3])
            for h in range(A_HEADS + 2):
                if h < A_HEADS:
                    act.wait_ge(amax_ready, h + 1)
                    if h >= 2:
                        act.wait_ge(tr_full[(GR["apt"] + h - 2) % 2], (GR["apt"] + h - 2) // 2 + 1)
                    for b in range(NB):
                        nc.scalar.activation(a_P[h % 2][:, b, :], mis[h % 2][:, b * T:(b + 1) * T], ACT.Exp,
                                             bias=a_nmx[:, 2 * (h % 2) + b:2 * (h % 2) + b + 1],
                                             accum_out=a_sum[:, 2 * (h % 2) + b:2 * (h % 2) + b + 1]).then_inc(ap_ready, 1)
                if 1 <= h <= A_HEADS and (GR["apt"] + h - 1) % 2 == 0:
                    if h >= 3:
                        act.wait_ge(o_full, h - 2)
                    copy_group(act, copy, GR["apt"] + h - 1, a_PT[(h - 1) % 2])
                if h >= 2:
                    act.wait_ge(o_full, h - 1)
                    nc.scalar.copy(actT_hi[:, h - 2, :], acc[(h - 2) % 4][:, 0:T]).then_inc(o_hi, 1)
            hi_weights(act, 23, range(3))
            with act.Fori(23, 25) as c:
                split_ahead(c)
            hi_weights(act, 25, [3])
            peer(1)

        @block.tensor
        def _(pe):
            mm, tp = nc.tensor.matmul, nc.tensor.transpose
            pe.sem_inc(w_used, 4)
            pe.sem_inc(v_used, NVS)
            pe.wait_ge(consts_in, 16)

            def norm(s, name, b):
                pe.wait_ge(xn_ready, 2 * s + b + 1)
                transposes(name, xn[b], b)

            def transposed_group(name, src, g):
                at, q = GR[name] + g, g % 4
                wait_bank(pe, at)
                for i in range(4):
                    f = 4 * q + i
                    last = tp(trb[at % 2][:, i * P:(i + 1) * P], src[:, f * P:(f + 1) * P], ident)
                last.then_inc(tr_full[at % 2], 1)

            def transposes(name, src, b, ready=None):
                for g in range(4 * b, 4 * b + 4):
                    if ready is not None:
                        pe.wait_ge(ready, g + 1)
                    transposed_group(name, src, g)
                wait_groups(pe, GR[name] + 4 * b, 4)

            def project(first, end, second=None, within=None):
                def quarter(c, par, b, j):
                    if j == 0:
                        pe.wait_ge(acc_out, c * 2 + (b + 1))
                    if b == 0:
                        pe.wait_ge(w_lo[j], c + 1)
                    for k in range(QK):
                        x_hi, x_lo = (t[:, QK * j + k, b * P:(b + 1) * P] for t in (actT_hi, actT_lo))
                        w_hi_k, w_lo_k = (t[j][:, k * CH:(k + 1) * CH] for t in (w_hi_of, w_lo_of))
                        for i, (xp, wp) in enumerate(((x_hi, w_hi_k), (x_hi, w_lo_k), (x_lo, w_hi_k))):
                            last = mm(acc[2 * par + b][:, :], xp, wp, start=(j == 0 and k == 0 and i == 0),
                                      stop=(j == 3 and k == QK - 1 and i == 2), skip_group_check=True)
                    if b == 1:
                        last.then_inc(w_used, 1)
                    elif j == 3:
                        last.then_inc(first_full, 1)

                def by_quarters(c, par):
                    for j in range(4):
                        for b in range(NB):
                            quarter(c, par, b, j)

                def by_blocks(c):
                    for b, j in ((0, 0), (0, 1), (0, 2), (1, 0), (0, 3), (1, 1), (1, 2), (1, 3)):
                        if (b, j) == (1, 3):
                            within()
                        quarter(c, c % 2, b, j)

                if second is not None:
                    for b, j in ((0, 0), (0, 1), (1, 0), (1, 1), (0, 2), (1, 2), (0, 3), (1, 3)):
                        if (b, j) == (1, 0):
                            second()
                        quarter(first, 0, b, j)
                    by_quarters(first + 1, 1)
                    first += 2
                stop = end - 2 if within is not None else end
                if first < stop:
                    with pe.Fori(first // 2, stop // 2) as pair:
                        for par in range(2):
                            by_quarters(pair * 2 + par, par)
                if within is not None:
                    by_quarters(end - 2, 0)
                    by_blocks(end - 1)

            def router(l, h, blocks=(0, 1)):
                n = h + (l * (HEADS + 1) + 1) if blocks != (0,) else l * (HEADS + 1)
                first = isinstance(h, int) and h == 0
                slots = wq0_slot if first else wq_slot
                for i in range(2):
                    if first:
                        pe.wait_ge(wq0_landed[i], 16 * (l + 1))
                    else:
                        pe.wait_ge(wq_landed[i], h * 16 + l * (HEADS - 1) * 16)
                for b in blocks:
                    for k in range(KT):
                        last = mm(mis[0][:, b * 2 * P:(b + 1) * 2 * P], actT[:, k, b * P:(b + 1) * P],
                                  slots[k // 8][:, k % 8, :], start=(k == 0), stop=(k == KT - 1),
                                  skip_group_check=True)
                last.then_inc(rq_full, 1)
                pe.wait_ge(rq_out, n + 1)
                for side in range(2):
                    for b in blocks:
                        i = 2 * side + b
                        last = tp(trb[0][:, i * P:(i + 1) * P],
                                  q_nat[:, (2 * b + side) * P:(2 * b + side + 1) * P], ident)
                last.then_inc(rt_full, 1)
                pe.wait_ge(rt_out, n + 1)
                for b in blocks:
                    for side in range(2):
                        i = 2 * b + side
                        last = mm(mis[1][:, i * P:(i + 1) * P], q_T[:, (2 * side + b) * P:(2 * side + b + 1) * P],
                                  keysT[:, side * P:(side + 1) * P], start=True, stop=True, skip_group_check=True)
                last.then_inc(sc_full, 1)

            def next_first(l):
                pe.wait_ge(keys_in, 32 * (l + 1))
                norm(2 * l + 1, f"n{2 * l + 1}", 0)
                router(l, 0, (0,))

            for b in range(NB):
                norm(0, "n0", b)
            project(0, 2)
            pe.wait_ge(wg_lo, 1)
            for k in range(KT):
                parts = ((w_gate_hi, actT_hi), (w_gate_lo, actT_hi), (w_gate_hi, actT_lo))
                for i, (wp, xp) in enumerate(parts):
                    last = mm(mis[0][0:16, 0:T], wp[:, k * 16:(k + 1) * 16], xp[:, k, :],
                              start=(k == 0 and i == 0), stop=(k == KT - 1 and i == 2))
            last.then_inc(gT_full, 1)
            pe.wait_ge(gT_ready, 1)
            for b in range(NB):
                last = tp(mis[1][:, b * 16:(b + 1) * 16], gatesT[:, b * P:(b + 1) * P], const[0:16, C_ID:C_ID + 16])
            last.then_inc(gates_full, 1)
            project(2, 4)
            pe.wait_ge(shared_in, 16)
            pe.wait_ge(ls_ready, 1)
            for b in range(NB):
                for d in range(2):
                    o = mis[1][:, b * 8 + d * 4:b * 8 + d * 4 + 4]
                    both = b == (1 if d == 0 else 0)
                    last = mm(o, tri[d], gls[:, b * 8 + d * 4:b * 8 + d * 4 + 4], start=True, stop=not both)
                    if both:
                        last = mm(o, ones, gls[:, (1 - b) * 8 + d * 4:(1 - b) * 8 + d * 4 + 4], start=False, stop=True)
            last.then_inc(cum_full, 1)
            pe.wait_ge(acc_out, 4 + 8)
            for g in range(8):
                wait_bank(pe, GR["qk"] + g)
                for i in range(4):
                    tile, b = 2 * g + i // 2, i % 2
                    last = tp(trb[(GR["qk"] + g) % 2][:, i * P:(i + 1) * P], mproj[:, b, tile * P:(tile + 1) * P], ident)
                last.then_inc(tr_full[(GR["qk"] + g) % 2], 1)
            project(4, 6)
            pe.wait_ge(a_ready, 1)
            wait_bank(pe, GR["a"])
            for b in range(NB):
                last = tp(trb[GR["a"] % 2][0:8, b * P:(b + 1) * P], ga[:, b * 8:(b + 1) * 8], ident)
            last.then_inc(tr_full[GR["a"] % 2], 1)
            wait_groups(pe, GR["a"], 1)
            for i in range(8):
                if i >= 2:
                    pe.wait_ge(bc_used, 2 * (i - 1))
                mm(mis[i % 2][:, 0:T], shared[0:8, M_SEL + i * P:M_SEL + (i + 1) * P], aT[:, :],
                   start=True, stop=True).then_inc(bc_full, 1)
            project(6, 8)
            wait_groups(pe, GR["qk"], 8)
            for i in range(8):
                head, b = i // 2, i % 2
                if i >= 2:
                    pe.wait_ge(s_used, 2 * (i - 1))
                elif i == 0:
                    pe.wait_ge(bc_used, 16)
                for d in range(M_QK // P):
                    last = mm(mis[i % 2][:, 0:T], m_qkT[:, 2 * head + d, b * P:(b + 1) * P],
                              m_qkT[:, NQK // P + 2 * head + d, :], start=(d == 0), stop=(d == M_QK // P - 1))
                last.then_inc(s_full, 1)
            project(8, 12)
            for h in range(M_HEADS):
                wait_bank(pe, GR["pt"] + h)
                pe.wait_ge(p_ready, 2 * h + 2)
                for i in range(4):
                    s, b = i // 2, i % 2
                    last = tp(trb[(GR["pt"] + h) % 2][:, i * P:(i + 1) * P], m_D(2 * h + b)[:, s * P:(s + 1) * P], ident)
                last.then_inc(tr_full[(GR["pt"] + h) % 2], 1)
            pe.wait_ge(acc_out, 4 + 24)
            wait_groups(pe, GR["pt"], M_HEADS)
            for i in range(8):
                b, head = i // 4, i % 4
                if i >= 4:
                    pe.wait_ge(h_out, i - 3)
                    pe.wait_ge(act_done, i - 3)
                for s in range(NB):
                    last = mm(acc[i % 4][:, :], m_PT[:, head, s, b * P:(b + 1) * P],
                              m_v[:, s, head * M_V:(head + 1) * M_V], start=(s == 0), stop=(s == NB - 1))
                last.then_inc(h_full, 1)
            transposes("h", m_h[:, 0], 0, h_ready)
            pe.wait_ge(h_out, 8)
            pe.wait_ge(act_done, 8)
            project(12, 16, second=lambda: transposes("h", m_h[:, 1], 1, h_ready), within=lambda: next_first(0))

            def peer(l):
                def seed(b):
                    for n in range(4):
                        mm(acc[n][:, :], ident, xb[b][:, n * CH:(n + 1) * CH], start=True, stop=False,
                           skip_group_check=True)

                def unit(gu, end, head=None):
                    for k in range(TOPK):
                        if k == 4 and head is not None:
                            router(l, head)
                        pe.wait_ge(diag_ready, gu * TOPK + (k + 1))
                        pe.wait_ge(v_landed[k % NVS], gu * 32 + (16 * (k // NVS) + 16))
                        for n in range(4):
                            last = mm(acc[n][:, :], diag[k % 4][:, :], v_slot[k % NVS][:, n * CH:(n + 1) * CH],
                                      start=False, stop=end and k == TOPK - 1, skip_group_check=True)
                        last.then_inc(v_used, 1)

                base = l * UNITS
                norm(2 * l + 1, f"n{2 * l + 1}", 1)
                router(l, 0, (1,))
                seed(0)
                with pe.Fori(0, HEADS - 1) as h:
                    unit(h + base, False, head=h + 1)
                unit(base + HEADS - 1, True)
                pe.wait_ge(x_out, 4 * (NB * l + 1))
                seed(1)
                with pe.Fori(0, HEADS - 1) as h:
                    unit(h + (base + HEADS), False)
                unit(base + UNITS - 1, True)

            peer(0)

            norm(2, "n2", 0)
            pe.wait_ge(x_out, 4 * NB)
            project(16, 22, second=lambda: norm(2, "n2", 1))
            pe.wait_ge(qk_ready, 10)
            for g in range(2):
                wait_bank(pe, GR["akT"] + g)
                for i in range(4):
                    kv, b = 2 * g + i // 2, i % 2
                    last = tp(trb[(GR["akT"] + g) % 2][:, i * P:(i + 1) * P],
                              aproj[:, b, (A_HEADS + kv) * P:(A_HEADS + kv + 1) * P], ident)
                last.then_inc(tr_full[(GR["akT"] + g) % 2], 1)
            for g in range(8):
                wait_bank(pe, GR["aqT"] + g)
                for i in range(4):
                    h, b = 2 * g + i // 2, i % 2
                    last = tp(trb[(GR["aqT"] + g) % 2][:, i * P:(i + 1) * P], aproj[:, b, h * P:(h + 1) * P], ident)
                last.then_inc(tr_full[(GR["aqT"] + g) % 2], 1)
            wait_groups(pe, GR["akT"], 10)
            pe.wait_ge(acc_out, 4 + 2 * 22)

            def a_scores(h):
                if h >= 2:
                    pe.wait_ge(ap_ready, 2 * (h - 1))
                for b in range(NB):
                    last = mm(mis[h % 2][:, b * T:(b + 1) * T], actT[:, h, b * P:(b + 1) * P],
                              a_kT[:, h // (A_HEADS // A_KV), :], start=True, stop=True, skip_group_check=True)
                last.then_inc(as_full, 1)

            a_scores(0)
            a_scores(1)
            for h in range(A_HEADS + 1):
                if h + 2 < A_HEADS:
                    a_scores(h + 2)
                if h < A_HEADS:
                    g = GR["apt"] + h
                    pe.wait_ge(an_ready, 2 * h + 2)
                    wait_bank(pe, g)
                    for i in range(4):
                        s, b = i // 2, i % 2
                        last = tp(trb[g % 2][:, i * P:(i + 1) * P], a_P[h % 2][:, b, s * P:(s + 1) * P], ident)
                    last.then_inc(tr_full[g % 2], 1)
                if h >= 1:
                    o = h - 1
                    wait_groups(pe, GR["apt"] + o, 1)
                    if o >= 4:
                        pe.wait_ge(o_out, o - 3)
                    kv = o // (A_HEADS // A_KV)
                    for s in range(NB):
                        last = mm(acc[o % 4][:, 0:T], aproj[:, s, (A_HEADS + A_KV + kv) * P:(A_HEADS + A_KV + kv + 1) * P],
                                  a_PT[o % 2][:, s, :], start=(s == 0), stop=(s == NB - 1))
                    last.then_inc(o_full, 1)
            pe.wait_ge(o_out, A_HEADS)
            project(22, 26, within=lambda: next_first(1))
            peer(1)

        @block.vector
        def _(dve):
            v = nc.vector
            st = Steps(dve, dve_done)
            did, need = st.did, st.need
            copy = v.tensor_copy
            dve.sem_inc(u_used, NU)
            dve.sem_inc(w_ready, 4)

            def norm(s, b, gain_no):
                dve.wait_ge(ssq_ready, 2 * s + b + 1)
                v.tensor_scalar(ms[:, b:b + 1], ssq[:, b:b + 1], 1.0 / D, EPS, ALU.mult, ALU.add).then_inc(ms_ready, 1)
                dve.wait_ge(rstd_ready, 2 * s + b + 1)
                dve.wait_ge(gain_in, 16 * (gain_no + 1))
                v.scalar_tensor_tensor(out=xn[b], in0=xb[b], scalar=rstd[:, b:b + 1], in1=gain[:, :],
                                       op0=ALU.mult, op1=ALU.mult).then_inc(xn_ready, 1)

            def copy_groups(name, groups, dst):
                for g in groups:
                    if (GR[name] + g) % 2:
                        copy_group(dve, copy, GR[name] + g, dst(g))

            def topk(l, gu, su, heads_seen):
                dve.wait_ge(sc_out, heads_seen)
                n = did(v.tensor_copy(scur[:, :], scores[:, bass.ds(su * (2 * P), 2 * P)]))
                need(n)
                S = [scur[:, i * P:(i + 1) * P] for i in range(2)]
                R = [srep[:, i * P:(i + 1) * P] for i in range(2)]
                V8 = [[t_val[:, i * 16 + 8 * r:i * 16 + 8 * r + 8] for r in range(2)] for i in range(2)]
                I8 = [[t_idx[:, i * 16 + 8 * r:i * 16 + 8 * r + 8] for r in range(2)] for i in range(2)]
                settle(dve)
                a = [did(v.max(V8[i][0], S[i])) for i in range(2)]
                c = []
                for i in range(2):
                    need(a[i])
                    settle(dve)
                    c.append(did(v.match_replace(R[i], V8[i][0], S[i], -3e38)))
                for i in range(2):
                    did(v.max_index(I8[i][0], V8[i][0], S[i]))
                e = []
                for i in range(2):
                    need(c[i])
                    settle(dve)
                    e.append(did(v.max(V8[i][1], R[i])))
                for i in range(2):
                    need(e[i])
                    settle(dve)
                    did(v.max_index(I8[i][1], V8[i][1], R[i]))
                m = st.n
                n = did(v.tensor_tensor(cand[:, :].rearrange("p (a b) -> p a b", a=16),
                                        t_val[:, 0:16].unsqueeze(2).to_broadcast([P, 16, 16]),
                                        t_val[:, 16:32].unsqueeze(1).to_broadcast([P, 16, 16]), ALU.add))
                need(st.loop + m)
                did(v.tensor_copy(t_idf[:, 0:16], t_idx[:, 0:16]))
                did(v.tensor_scalar(t_idf[:, 16:32], t_idx[:, 16:32], float(l * EXPERTS), None, ALU.add))
                need(n)
                settle(dve)
                need(did(v.max(c_top[:, 0:8], cand[:, :])))
                did(v.tensor_scalar(negmax[:, :], c_top[:, 0:1], -1.0, None, ALU.mult))
                n = did(v.match_replace(crep[:, :], c_top[:, 0:8], cand[:, :], -3e38))
                did(v.max_index(c_pos[:, 0:8], c_top[:, 0:8], cand[:, :]))
                need(n)
                settle(dve)
                v.max(c_top[:, 8:16], crep[:, :]).then_inc(top_ready, 1)
                dve.wait_ge(top_ready, gu + 1)
                settle(dve)
                need(did(v.max_index(c_pos[:, 8:16], c_top[:, 8:16], crep[:, :])))
                did(v.tensor_scalar(c_ab[:, 0:16], c_pos[:, :], 4, None, ALU.logical_shift_right))
                need(did(v.tensor_scalar(c_ab[:, 16:32], c_pos[:, :], 15, None, ALU.bitwise_and)))
                oh = onehot[:, :].rearrange("p (j a) -> p j a", a=16)
                need(did(v.tensor_tensor(oh, c_ab[:, :].unsqueeze(2).to_broadcast([P, 32, 16]),
                                         iota.unsqueeze(1).to_broadcast([P, 32, 16]), ALU.is_equal)))
                oh4 = onehot[:, :].rearrange("p (s j a) -> p s j a", s=2, a=16)
                ids = t_idf[:, :].rearrange("p (s a) -> p s a", s=2).unsqueeze(2).to_broadcast([P, 2, 16, 16])
                need(did(v.tensor_tensor(oh4, oh4, ids, ALU.mult)))
                need(did(v.tensor_reduce(sel_if[:, :], oh, AX.X, ALU.add)))
                if not isinstance(gu, int) or gu > 0:
                    dve.wait_ge(idx_taken, gu)
                v.scalar_tensor_tensor(out=idx_next[:, :], in0=sel_if[:, 0:16], scalar=float(P),
                                       in1=sel_if[:, 16:32], op0=ALU.mult, op1=ALU.add).then_inc(idx_ready, 1)
                dve.wait_ge(gexp_ready, gu + 1)
                need(did(v.reciprocal(g_rec[:, :], g_sum[:, :])))
                did(v.tensor_scalar(gate_next[:, :], g_exp[:, :], g_rec[:, :], None, ALU.mult))

            def add_output(first, l):
                stage, gain_no = 2 * l + 1, 2 * l + 2
                for c in range(4):
                    for b in range(NB):
                        if b == 0:
                            dve.wait_ge(first_full, first + c + 1)
                        else:
                            dve.wait_ge(w_used, 4 + 4 * (first + c) + 4)
                        at = xb[b][:, c * CH:(c + 1) * CH]
                        v.tensor_tensor(at, acc[2 * (c % 2) + b][:, :], at, ALU.add).then_inc(acc_out, 1)
                        if c == 3:
                            norm(stage, b, gain_no)
                            copy_groups(f"n{stage}", range(4 * b, 4 * b + 4), norm_dst)
                        if c == 3 and b == 0:
                            topk(l, l * UNITS, 0, l * (HEADS + 1) + 1)

            dve.wait_ge(consts_in, 16)
            for b in range(NB):
                norm(0, b, 0)
            lo_groups(dve, "n0", range(8))
            lo_weights(dve, v, 0, range(4))
            dve.wait_ge(wg_hi, 1)
            v.tensor_tensor(w_gate_lo[:, :], w_gate[:, :], w_gate_hi[:, :].bitcast(F32),
                            ALU.subtract).then_inc(wg_lo, 1)
            dve.wait_ge(gT_full, 1)
            copy(gatesT[:, :], mis[0][0:16, 0:T]).then_inc(gT_ready, 1)
            dve.wait_ge(gates_full, 1)
            n = did(v.tensor_tensor(g_sb[:, :].rearrange("p (b g) -> p b g", b=NB),
                                    mis[1][:, 0:32].rearrange("p (b g) -> p b g", b=NB),
                                    bias[:, :].unsqueeze(1).to_broadcast([P, NB, 16]), ALU.add))
            need(n)
            g4 = g_sb[:, :].rearrange("p (b d t h) -> p (b d) t h", b=NB, d=2, t=2)
            g_i, g_f = g4[:, :, 0, :], g4[:, :, 1, :]

            def w4(t):
                return t[:, 0:16].rearrange("p (x h) -> p x h", h=4)
            v.scalar_tensor_tensor(out=w4(gf), in0=g_f, scalar=-1.0, in1=g_f, op0=ALU.mult, op1=ALU.max).then_inc(exp_in, 1)
            dve.wait_ge(exp_out, 1)
            need(did(v.tensor_scalar(gd[:, 0:16], ge[:, 0:16], 2.0, None, ALU.add)))
            need(did(v.reciprocal(gr[:, 0:16], gd[:, 0:16])))
            need(did(v.tensor_tensor(gz[:, 0:16], ge[:, 0:16], gr[:, 0:16], ALU.mult)))
            need(did(v.tensor_tensor(gz2[:, 0:16], gz[:, 0:16], gz[:, 0:16], ALU.mult)))
            need(did(v.tensor_scalar(gp[:, 0:16], gz2[:, 0:16], 1.0 / 15, None, ALU.mult)))
            for c in (13, 11, 9, 7, 5, 3):
                need(did(v.scalar_tensor_tensor(out=gp[:, 0:16], in0=gp[:, 0:16], scalar=1.0 / c, in1=gz2[:, 0:16],
                                                op0=ALU.add, op1=ALU.mult)))
            need(did(v.scalar_tensor_tensor(out=gp[:, 0:16], in0=gp[:, 0:16], scalar=1.0, in1=gz[:, 0:16],
                                            op0=ALU.add, op1=ALU.mult)))
            need(did(v.tensor_scalar(w4(gd), g_f, 0.0, None, ALU.min)))
            v.scalar_tensor_tensor(out=gls[:, :], in0=gp[:, 0:16], scalar=-2.0, in1=gd[:, 0:16],
                                   op0=ALU.mult, op1=ALU.add).then_inc(ls_ready, 1)
            dve.wait_ge(cum_full, 1)
            did(v.tensor_copy(gB[:, :], mis[1][:, 0:16]))
            v.tensor_tensor(w4(ga), g_i, w4(mis[1]), ALU.subtract).then_inc(a_ready, 1)
            for g in range(8):
                if (GR["qk"] + g) % 2:
                    copy_group(dve, copy, GR["qk"] + g, qkT_dst(g))
            dve.wait_ge(shared_in, 16)
            for i in range(8):
                dve.wait_ge(bc_full, i + 1)
                for b in range(NB):
                    mask = shared[:, M_MASK + (2 * (i // 4) + b) * 256:M_MASK + (2 * (i // 4) + b + 1) * 256]
                    v.tensor_tensor_reduce(m_D(2 * i + b), mis[i % 2][:, 0:T], mask, 1.0, 0.0, ALU.add,
                                           ALU.max, m_M[:, 2 * i + b:2 * i + b + 1]).then_inc(bc_used, 1)
            dve.wait_ge(bc_used, 16)
            did(v.tensor_scalar(m_negM[:, :], m_M[:, :], -1.0, None, ALU.mult))
            need(st.n)
            v.tensor_tensor(m_nm[:, :].rearrange("p (x b) -> p x b", b=NB),
                            m_negM[:, :].rearrange("p (x b) -> p x b", b=NB),
                            gB[:, :].rearrange("p (b x) -> p x b", b=NB), ALU.subtract).then_inc(negm_ready, 1)
            for i in range(8):
                head, b = i // 2, i % 2
                dve.wait_ge(s_full, i + 1)
                for d in range(2):
                    k = (d * M_HEADS + head) * 2 + b
                    dve.wait_ge(decay_ready, k + 1)
                    v.tensor_tensor_reduce(m_D(k), mis[i % 2][:, 0:T], m_D(k), M_QK ** -0.5, 0.0,
                                           ALU.mult, ALU.add, m_den[:, k:k + 1]).then_inc(s_used, 1)
            dve.wait_ge(s_used, 16)
            dve.wait_ge(en_ready, 1)
            need(did(v.scalar_tensor_tensor(out=m_dn[:, :], in0=m_den[:, :], scalar=-1.0, in1=m_den[:, :],
                                            op0=ALU.mult, op1=ALU.max)))
            need(did(v.tensor_tensor(m_dn[:, :], m_dn[:, :], m_en[:, :], ALU.max)))
            need(did(v.reciprocal(m_rr[:, :], m_dn[:, :])))
            for i in range(8):
                did(v.tensor_scalar(m_D(i), m_D(i), m_rr[:, i:i + 1], None, ALU.mult))
            for i in range(8):
                need(st.n - 7 + i)
                v.scalar_tensor_tensor(out=m_D(i), in0=m_D(8 + i), scalar=m_rr[:, 8 + i:9 + i],
                                       in1=m_D(i), op0=ALU.mult, op1=ALU.add).then_inc(p_ready, 1)
            for h in range(M_HEADS):
                if (GR["pt"] + h) % 2:
                    copy_group(dve, copy, GR["pt"] + h, m_PT[:, h, :, :])
            dve.wait_ge(gain_in, 32)
            dve.wait_ge(acc_out, 4 + 24)
            for b in range(NB):
                did(v.tensor_tensor(m_o[:, b, :], m_o[:, b, :], gain[:, :], ALU.mult))
            gated = st.n

            def head_ms(b):
                dve.wait_ge(act_done, 4 * b + 4)
                c = slice(4 * b, 4 * b + 4)
                v.tensor_scalar(h_ms[:, c], h_ssq[:, c], 1.0 / M_V, EPS, ALU.mult, ALU.add).then_inc(msh_ready, 1)

            head_ms(0)
            for b in range(NB):
                dve.wait_ge(h_out, 4 * b + 4)
                dve.wait_ge(rh_ready, b + 1)
                need(gated)
                for head in range(M_HEADS):
                    at = m_h[:, b, head * M_V:(head + 1) * M_V]
                    i = 4 * b + head
                    v.scalar_tensor_tensor(out=at, in0=at, scalar=h_r[:, i:i + 1],
                                           in1=m_o[:, b, head * M_V:(head + 1) * M_V],
                                           op0=ALU.mult, op1=ALU.mult).then_inc(h_ready, 1)
                if b == 0:
                    head_ms(1)
                lo_groups(dve, "h", range(4 * b, 4 * b + 4))
            add_output(12, 0)

            def peer(l):
                def unit(b, gu, nxt, groups=GROUPS):
                    start = st.loop + st.n
                    need(start)
                    dve.wait_ge(w_ready, gu * 4 + (EXTRA * l + 4))
                    did(v.tensor_copy(gate_cur[:, :], gate_next[:, :]))

                    def dot(k):
                        dve.wait_ge(u_landed[k % NU], gu * 64 + (16 * (k // NU) + 16))
                        v.tensor_tensor_reduce(u_slot[k % NU], u_slot[k % NU], xn[b], 1.0, 0.0, ALU.mult, ALU.add,
                                               dots[:, k:k + 1]).then_inc(u_used, 1)

                    def pre(k0, k1):
                        c = slice(k0, k1)
                        dve.wait_ge(u_used, gu * TOPK + (NU + k1))
                        need(did(v.tensor_tensor(e_x2[:, c], dots[:, c], dots[:, c], ALU.mult)))
                        need(did(v.tensor_scalar(e_t[:, c], e_x2[:, c], GELU_A, 1.0, ALU.mult, ALU.add)))
                        v.tensor_tensor(e_in[:, c], e_t[:, c], dots[:, c], ALU.mult).then_inc(tanh_in, 1)

                    def post(j):
                        c = slice(*groups[j])
                        dve.wait_ge(tanh_out, gu * 4 + (EXTRA * l + j + 1))
                        need(did(v.scalar_tensor_tensor(out=e_p[:, c], in0=e_th[:, c], scalar=1.0, in1=dots[:, c],
                                                        op0=ALU.add, op1=ALU.mult)))
                        v.scalar_tensor_tensor(out=e_w[:, c], in0=e_p[:, c], scalar=0.5, in1=gate_cur[:, c],
                                               op0=ALU.mult, op1=ALU.mult).then_inc(w_ready, 1)

                    begun = {k0: j for j, (k0, k1) in enumerate(groups)}
                    ended = {k1: j for j, (k0, k1) in enumerate(groups)}
                    for k in range(TOPK):
                        dot(k)
                        single = groups[begun.get(k, 0)] == (k, k + 1)
                        if not single and k in begun and k:
                            post(begun[k] - 1)
                        if k + 1 in ended:
                            j = ended[k + 1]
                            pre(*groups[j])
                            if single:
                                if groups[j - 1][1] - groups[j - 1][0] > 1:
                                    post(j - 1)
                                post(j)
                        if k == 8 and nxt:
                            topk(l, *nxt)
                    if not single:
                        post(len(groups) - 1)

                base = l * UNITS
                seen = l * (HEADS + 1) + 1
                UNIT_STEPS = 39
                with dve.Fori(0, HEADS - 1) as h:
                    at = st.n
                    st.loop = h * UNIT_STEPS
                    unit(0, h + base, (h + (base + 1), h + 1, h + (seen + 2)))
                    assert st.n - at == UNIT_STEPS, st.n - at
                st.loop = 0
                st.n = at + UNIT_STEPS * (HEADS - 1)
                unit(0, base + HEADS - 1, (base + HEADS, HEADS, seen + HEADS))
                with dve.Fori(0, HEADS - 1) as h:
                    at = st.n
                    st.loop = h * UNIT_STEPS
                    unit(1, h + (base + HEADS), (h + (base + HEADS + 1), h + (HEADS + 1), seen + HEADS))
                    assert st.n - at == UNIT_STEPS, st.n - at
                st.loop = 0
                st.n = at + UNIT_STEPS * (HEADS - 1)
                unit(1, base + UNITS - 1, None, LAST_GROUPS)

            peer(0)

            norm(2, 0, 3)
            lo_groups(dve, "n2", range(0, 2))
            lo_weights(dve, v, 16, [0])
            lo_groups(dve, "n2", range(2, 4))
            norm(2, 1, 3)
            lo_weights(dve, v, 16, [1])
            lo_groups(dve, "n2", range(4, 8))
            dve.wait_ge(qkg_in, 32)
            need(did(v.tensor_scalar(qkgain[:, 0:P], qkgain[:, 0:P], DH ** -0.5, None, ALU.mult)))
            HC = CH // DH
            for c in range(5):
                par = c % 2
                dve.wait_ge(sq_ready, 2 * c + 2)
                need(did(v.tensor_reduce(q_ssq[:, :], a_sq.rearrange("p (h d) -> p h d", d=DH), AX.X, ALU.add)))
                v.tensor_scalar(q_ms[:, :], q_ssq[:, :], 1.0 / DH, EPS, ALU.mult, ALU.add).then_inc(msq_ready, 1)
                dve.wait_ge(rq_ready, c + 1)
                g = qkgain[:, 0:P] if c < 4 else qkgain[:, P:2 * P]
                s0 = st.n
                for b in range(NB):
                    v.tensor_tensor(a_y[:, b], acc[2 * par + b][:, :].rearrange("p (h d) -> p h d", d=DH),
                                    q_r[:, b * HC:(b + 1) * HC].unsqueeze(2).to_broadcast([P, HC, DH]),
                                    ALU.mult).then_inc(acc_out, 1)
                for b in range(NB):
                    dve.wait_ge(acc_out, 4 + 2 * (M_CHUNKS + c) + b + 1)
                    did(v.tensor_tensor(a_y[:, b], a_y[:, b], g.unsqueeze(1).to_broadcast([P, HC, DH]), ALU.mult))
                for b in range(NB):
                    need(s0 + 1 + b)
                    cos = const[:, C_COS + b * P:C_COS + (b + 1) * P].unsqueeze(1).to_broadcast([P, HC, DH])
                    sin = const[:, C_SIN + b * 64:C_SIN + (b + 1) * 64].unsqueeze(1).to_broadcast([P, HC, 64])
                    y2 = a_y[:, b].rearrange("p h (e two) -> p h e two", two=2)
                    t2 = a_t2[:, b].rearrange("p h (e two) -> p h e two", two=2)
                    did(v.tensor_tensor(a_t1[:, b], a_y[:, b], cos, ALU.mult))
                    did(v.scalar_tensor_tensor(out=t2[:, :, :, 0], in0=y2[:, :, :, 1], scalar=-1.0, in1=sin,
                                               op0=ALU.mult, op1=ALU.mult))
                    did(v.tensor_tensor(t2[:, :, :, 1], y2[:, :, :, 0], sin, ALU.mult))
                for b in range(NB):
                    need(s0 + 2 + 3 * (b + 1))
                    v.tensor_tensor(aproj[:, b, c * CH:(c + 1) * CH].rearrange("p (h d) -> p h d", d=DH),
                                    a_t1[:, b], a_t2[:, b], ALU.add).then_inc(qk_ready, 1)
            for g in range(2):
                if (GR["akT"] + g) % 2:
                    copy_group(dve, copy, GR["akT"] + g, a_kT[:, 2 * g:2 * g + 2, :])
            for g in range(8):
                if (GR["aqT"] + g) % 2:
                    copy_group(dve, copy, GR["aqT"] + g, actT[:, 2 * g:2 * g + 2, :])
            def maxima(h):
                c = slice(2 * (h % 2), 2 * (h % 2) + 2)
                dve.wait_ge(as_full, h + 1)
                need(did(v.tensor_reduce(a_mx[:, c], mis[h % 2][:, :].rearrange("p (b s) -> p b s", b=NB),
                                         AX.X, ALU.max)))
                v.tensor_scalar(a_nmx[:, c], a_mx[:, c], -1.0, None, ALU.mult).then_inc(amax_ready, 1)

            def output_lo(h):
                dve.wait_ge(o_hi, h + 1)
                v.tensor_tensor(actT_lo[:, h, :], acc[h % 4][:, 0:T], actT_hi[:, h, :].bitcast(F32),
                                ALU.subtract).then_inc(o_out, 1)

            maxima(0)
            for h in range(A_HEADS + 1):
                if h + 1 < A_HEADS:
                    maxima(h + 1)
                if h < A_HEADS:
                    c = slice(2 * (h % 2), 2 * (h % 2) + 2)
                    dve.wait_ge(ap_ready, 2 * h + 2)
                    need(did(v.reciprocal(a_rs[:, c], a_sum[:, c])))
                    for b in range(NB):
                        v.tensor_scalar(a_P[h % 2][:, b, :], a_P[h % 2][:, b, :],
                                        a_rs[:, 2 * (h % 2) + b:2 * (h % 2) + b + 1], None, ALU.mult).then_inc(an_ready, 1)
                if h >= 1 and (GR["apt"] + h - 1) % 2:
                    if h >= 3:
                        dve.wait_ge(o_full, h - 2)
                    copy_group(dve, copy, GR["apt"] + h - 1, a_PT[(h - 1) % 2])
                if h >= 2:
                    output_lo(h - 2)
            output_lo(A_HEADS - 1)
            add_output(22, 1)
            peer(1)


_INS = ["x", "ln_mix", "ln_ffn", "mlstm_w_in", "mlstm_gate_bias", "mlstm_head_norm", "mlstm_w_out", "attn_w_in",
        "attn_q_norm", "attn_k_norm", "attn_w_out", "peer_wq", "peer_k1", "peer_k2", "peer_u", "peer_v"]


def kernel(**inputs):
    import numpy as _np
    import concourse.bacc as _bacc
    from concourse import mybir as _mybir
    from concourse.bass_utils import run_bass_kernel_spmd as _run

    nc = _bacc.Bacc("TRN2", target_bir_lowering=False, num_devices=1)
    arrays, args = {}, []
    for name in ["consts"] + _INS:
        if name == "consts":
            a = constants()
        else:
            a = _np.asarray(inputs[name])
            if name in ("peer_k1", "peer_k2"):
                a = a.transpose(0, 2, 1)
            a = _np.ascontiguousarray(a)
        arrays[f"in_{name}_dram"] = a
        args.append(nc.dram_tensor(f"in_{name}_dram", a.shape, _mybir.dt.from_np(a.dtype), kind="ExternalInput").ap())
    shape = _np.asarray(inputs["x"]).shape
    args.append(nc.dram_tensor("out_dram", shape, _mybir.dt.float32, kind="ExternalOutput").ap())
    trunk_kernel(nc, *args)
    r = _run(nc, [arrays], core_ids=[0])
    return r.results[0]["out_dram"]
```
